# Optimizing a Trainium2 kernel written in Bass

```python
import math
import jax, jax.numpy as jnp
from jax import lax
import numpy as np

D_MODEL = 1024
BATCH = 1
SEQ = 256
DEPTH = 1

HG_HEADS = 4
HG_DK = 128
HG_DV = 128
HG_KEY_WIDTH = HG_HEADS * HG_DK
HG_WIDTH = HG_HEADS * HG_DV
HG_CHUNK = 64

MB_HEADS = 8
MB_DH = 64
MB_WIDTH = MB_HEADS * MB_DH
MB_BLOCK = 256
MB_TOPK = 3
MB_QCHUNK = 16

REL_BUCKETS = 32
REL_MAX_DIST = 128

N_GROUPS = 4
EXPERTS_PER_GROUP = 8
N_EXPERTS = N_GROUPS * EXPERTS_PER_GROUP
TOP_K = 2
EXPERT_HIDDEN = 512
MOE_BLOCK = 128

DN_ALPHA = (2.0 * DEPTH) ** 0.25
DN_BETA = (8.0 * DEPTH) ** -0.25
NORM_EPS = 1e-5

IN_SIZES = (HG_KEY_WIDTH, HG_KEY_WIDTH, HG_WIDTH, HG_WIDTH, MB_WIDTH, MB_WIDTH, MB_WIDTH, D_MODEL, D_MODEL)
IN_COLS = sum(IN_SIZES)


def layer_norm(x, g, b):
    xf = x.astype(jnp.float32)
    mu = jnp.mean(xf, axis=-1, keepdims=True)
    xc = xf - mu
    var = jnp.mean(xc * xc, axis=-1, keepdims=True)
    return (xc * lax.rsqrt(var + NORM_EPS) * g.astype(jnp.float32) + b.astype(jnp.float32)).astype(x.dtype)

def hgrn2_mixer(q, f_logit, i, g, lb, norm_g):
    B, S, _ = q.shape
    nc = S // HG_CHUNK
    f32 = jnp.float32
    lb = lb.astype(f32)
    z = f_logit.astype(f32)
    log_f = jnp.log(lb + (1.0 - lb) * jax.nn.sigmoid(z))
    k = (1.0 - lb) * jax.nn.sigmoid(-z)
    qf = jax.nn.silu(q.astype(f32))
    vf = i.astype(f32)

    def to_chunks(t, dh):
        return t.reshape(B, nc, HG_CHUNK, HG_HEADS, dh).transpose(1, 0, 3, 2, 4)

    causal = jnp.tril(jnp.ones((HG_CHUNK, HG_CHUNK), dtype=bool))

    def chunk_step(state, inp):
        qc, kc, vc, lfc = inp
        b = jnp.cumsum(lfc, axis=2)
        o_inter = jnp.einsum('bhtk,bhkv->bhtv', qc * jnp.exp(b), state)
        rel = b[:, :, :, None, :] - b[:, :, None, :, :]
        decay = jnp.exp(jnp.where(causal[:, :, None], rel, -jnp.inf))
        scores = jnp.einsum('bhtk,bhtsk,bhsk->bhts', qc, decay, kc)
        o_intra = jnp.einsum('bhts,bhsv->bhtv', scores, vc)
        b_end = b[:, :, -1:, :]
        state = (jnp.exp(b_end[:, :, 0, :])[..., None] * state
                 + jnp.einsum('bhsk,bhsv->bhkv', kc * jnp.exp(b_end - b), vc))
        return state, o_inter + o_intra

    s0 = jnp.zeros((B, HG_HEADS, HG_DK, HG_DV), f32)
    _, o = lax.scan(chunk_step, s0, (to_chunks(qf, HG_DK), to_chunks(k, HG_DK),
                                     to_chunks(vf, HG_DV), to_chunks(log_f, HG_DK)))
    o = o.transpose(1, 0, 3, 2, 4).reshape(B, S, HG_HEADS, HG_DV)
    o = o * lax.rsqrt(jnp.mean(o * o, axis=-1, keepdims=True) + NORM_EPS)
    o = o.reshape(B, S, HG_WIDTH) * norm_g.astype(f32) * jax.nn.silu(g.astype(f32))
    return o.astype(q.dtype)

def t5_bucket(dist):
    max_exact = REL_BUCKETS // 2
    d = jnp.maximum(dist, 1).astype(jnp.float32)
    log_part = max_exact + (jnp.log(d / max_exact) / math.log(REL_MAX_DIST / max_exact)
                            * (REL_BUCKETS - max_exact)).astype(jnp.int32)
    return jnp.where(dist < max_exact, dist, jnp.minimum(log_part, REL_BUCKETS - 1))

def moba_mixer(q, k, v, rel_bias):
    B, S, _ = q.shape
    f32 = jnp.float32
    nb = -(-S // MB_BLOCK)
    s_pad = nb * MB_BLOCK
    k_sel = min(MB_TOPK, nb)
    scale = MB_DH ** -0.5

    def to_heads(t):
        t = jnp.pad(t, ((0, 0), (0, s_pad - S), (0, 0)))
        return t.reshape(B, s_pad, MB_HEADS, MB_DH).transpose(0, 2, 1, 3)

    qh, kh, vh = to_heads(q), to_heads(k), to_heads(v)
    kb = kh.reshape(B, MB_HEADS, nb, MB_BLOCK, MB_DH)
    vb = vh.reshape(B, MB_HEADS, nb, MB_BLOCK, MB_DH)
    k_mean = jnp.mean(kb, axis=3)
    gate = jnp.einsum('bhsd,bhnd->bhsn', qh, k_mean).astype(f32)
    pos = jnp.arange(s_pad)
    fully_past = jnp.arange(nb)[None, :] < (pos // MB_BLOCK)[:, None]
    gate = jnp.where(fully_past, gate, -jnp.inf)
    top_val, top_idx = lax.top_k(gate, k_sel)
    top_ok = jnp.isfinite(top_val)

    rb = rel_bias.astype(f32).T
    b_ix = jnp.arange(B)[:, None, None, None]
    h_ix = jnp.arange(MB_HEADS)[None, :, None, None]

    def attend(c):
        t0 = c * MB_QCHUNK
        tq = t0 + jnp.arange(MB_QCHUNK)
        qc = lax.dynamic_slice_in_dim(qh, t0, MB_QCHUNK, axis=2)
        idx = lax.dynamic_slice_in_dim(top_idx, t0, MB_QCHUNK, axis=2)
        ok = lax.dynamic_slice_in_dim(top_ok, t0, MB_QCHUNK, axis=2)
        kg = kb[b_ix, h_ix, idx]
        vg = vb[b_ix, h_ix, idx]
        kpos = idx[..., None] * MB_BLOCK + jnp.arange(MB_BLOCK)
        bucket = t5_bucket(tq[None, None, :, None, None] - kpos)
        s_past = (jnp.einsum('bhqd,bhqjkd->bhqjk', qc, kg).astype(f32) * scale
                  + rb[h_ix[..., None], bucket])
        s_past = jnp.where(ok[..., None], s_past, -jnp.inf).reshape(B, MB_HEADS, MB_QCHUNK, k_sel * MB_BLOCK)
        j0 = (t0 // MB_BLOCK) * MB_BLOCK
        k_own = lax.dynamic_slice_in_dim(kh, j0, MB_BLOCK, axis=2)
        v_own = lax.dynamic_slice_in_dim(vh, j0, MB_BLOCK, axis=2)
        dist_own = tq[:, None] - (j0 + jnp.arange(MB_BLOCK))[None, :]
        s_own = (jnp.einsum('bhqd,bhkd->bhqk', qc, k_own).astype(f32) * scale
                 + rb[:, t5_bucket(jnp.maximum(dist_own, 0))])
        s_own = jnp.where(dist_own >= 0, s_own, -jnp.inf)
        p = jax.nn.softmax(jnp.concatenate([s_past, s_own], axis=-1), axis=-1)
        p_past = p[..., :k_sel * MB_BLOCK].reshape(B, MB_HEADS, MB_QCHUNK, k_sel, MB_BLOCK).astype(vg.dtype)
        p_own = p[..., k_sel * MB_BLOCK:].astype(v_own.dtype)
        return (jnp.einsum('bhqjk,bhqjkd->bhqd', p_past, vg)
                + jnp.einsum('bhqk,bhkd->bhqd', p_own, v_own))

    o = lax.map(attend, jnp.arange(s_pad // MB_QCHUNK))
    o = o.transpose(1, 0, 3, 2, 4).reshape(B, s_pad, MB_WIDTH)[:, :S]
    return o

def hier_moe(x, w_group, b_group, w_expert, b_expert, w_gate_up, w_down):
    B, S, D = x.shape
    n_tok = B * S
    n_asg = n_tok * TOP_K
    f32 = jnp.float32
    xt = x.reshape(n_tok, D)
    g_logits = (xt @ w_group + b_group).astype(f32)
    grp = jnp.argmax(g_logits, axis=-1)
    p_grp = jnp.take_along_axis(jax.nn.softmax(g_logits, axis=-1), grp[:, None], axis=1)
    e_logits = (xt @ w_expert + b_expert).astype(f32).reshape(n_tok, N_GROUPS, EXPERTS_PER_GROUP)
    e_in_grp = jnp.take_along_axis(e_logits, grp[:, None, None], axis=1)[:, 0]
    top_v, top_i = lax.top_k(e_in_grp, TOP_K)
    weights = (jax.nn.softmax(top_v, axis=-1) * p_grp).reshape(n_asg)
    expert = (grp[:, None] * EXPERTS_PER_GROUP + top_i).reshape(n_asg)
    token = jnp.repeat(jnp.arange(n_tok), TOP_K)
    order = jnp.argsort(expert)
    e_s, tok_s, w_s = expert[order], token[order], weights[order]
    counts = jax.ops.segment_sum(jnp.ones((n_asg,), jnp.int32), expert, num_segments=N_EXPERTS)
    starts = jnp.cumsum(counts) - counts
    padded = (counts + MOE_BLOCK - 1) // MOE_BLOCK * MOE_BLOCK
    pad_end = jnp.cumsum(padded)
    pad_start = pad_end - padded
    dest = pad_start[e_s] + jnp.arange(n_asg) - starts[e_s]
    n_blk = -(-n_asg // MOE_BLOCK) + N_EXPERTS
    n_rows = n_blk * MOE_BLOCK
    x_buf = jnp.zeros((n_rows, D), x.dtype).at[dest].set(xt[tok_s])
    blk_expert = jnp.minimum(jnp.searchsorted(pad_end, jnp.arange(n_blk) * MOE_BLOCK, side='right'),
                             N_EXPERTS - 1)

    def expert_block(args):
        xb, e = args
        gate, up = jnp.split(xb @ w_gate_up[e], 2, axis=-1)
        return (jax.nn.silu(gate) * up) @ w_down[e]

    y_buf = lax.map(expert_block, (x_buf.reshape(n_blk, MOE_BLOCK, D), blk_expert)).reshape(n_rows, D)
    y = jnp.zeros((n_tok, D), x.dtype).at[tok_s].add(y_buf[dest] * w_s[:, None].astype(x.dtype))
    return y.reshape(B, S, D)

def first_inputs(seed: int = 0) -> dict:
    key = jax.random.key(seed)
    ks = jax.random.split(key, 20)
    f32 = jnp.float32
    L = DEPTH

    def normal(k, shape, std):
        return jax.random.normal(k, shape, f32) * std

    col_scale = jnp.concatenate([jnp.full((n,), s, f32) for n, s in
                                 zip(IN_SIZES, (1.0, 1.0, DN_BETA, 1.0, 1.0, 1.0, DN_BETA, 1.0, 1.0))])
    return {
        'x': normal(ks[0], (BATCH, SEQ, D_MODEL), 1.0),
        'w_in': normal(ks[1], (L, D_MODEL, IN_COLS), D_MODEL ** -0.5) * col_scale,
        'b_in': normal(ks[2], (L, IN_COLS), 0.02),
        'lb_logits': normal(ks[3], (L + 1, HG_KEY_WIDTH), 0.5),
        'hg_norm_g': 1.0 + normal(ks[4], (L, HG_WIDTH), 0.1),
        'rel_bias': normal(ks[5], (REL_BUCKETS, MB_HEADS), 0.5),
        'w_proj_a': normal(ks[6], (L, HG_WIDTH, D_MODEL), DN_BETA * HG_WIDTH ** -0.5),
        'w_proj_b': normal(ks[7], (L, MB_WIDTH, D_MODEL), DN_BETA * MB_WIDTH ** -0.5),
        'w_out': normal(ks[8], (L, D_MODEL, D_MODEL), DN_BETA * D_MODEL ** -0.5),
        'ln1_g': 1.0 + normal(ks[9], (L, D_MODEL), 0.1),
        'ln1_b': normal(ks[10], (L, D_MODEL), 0.02),
        'w_group': normal(ks[11], (L, D_MODEL, N_GROUPS), D_MODEL ** -0.5),
        'b_group': normal(ks[12], (L, N_GROUPS), 0.01),
        'w_expert': normal(ks[13], (L, D_MODEL, N_EXPERTS), D_MODEL ** -0.5),
        'b_expert': normal(ks[14], (L, N_EXPERTS), 0.01),
        'w_gate_up': normal(ks[15], (L, N_EXPERTS, D_MODEL, 2 * EXPERT_HIDDEN), D_MODEL ** -0.5),
        'w_down': normal(ks[16], (L, N_EXPERTS, EXPERT_HIDDEN, D_MODEL), DN_BETA * EXPERT_HIDDEN ** -0.5),
        'ln2_g': 1.0 + normal(ks[17], (L, D_MODEL), 0.1),
        'ln2_b': normal(ks[18], (L, D_MODEL), 0.02),
    }

def first_block(x, w_in, b_in, lb_logits, hg_norm_g, rel_bias, w_proj_a, w_proj_b, w_out, ln1_g, ln1_b,
              w_group, b_group, w_expert, b_expert, w_gate_up, w_down, ln2_g, ln2_b):
    split_at = [int(s) for s in np.cumsum(IN_SIZES)[:-1]]
    lower_bounds = jnp.cumsum(jax.nn.softmax(lb_logits.astype(jnp.float32), axis=0), axis=0)
    for l in range(DEPTH):
        h = x
        proj = h @ w_in[l] + b_in[l]
        hg_q, hg_f, hg_i, hg_g, mb_q, mb_k, mb_v, gate_a, gate_b = jnp.split(proj, split_at, axis=-1)
        y_a = hgrn2_mixer(hg_q, hg_f, hg_i, hg_g, lower_bounds[l], hg_norm_g[l]) @ w_proj_a[l]
        y_b = moba_mixer(mb_q, mb_k, mb_v, rel_bias) @ w_proj_b[l]
        mixed = (jax.nn.sigmoid(gate_a) * y_a + jax.nn.sigmoid(gate_b) * y_b) @ w_out[l]
        x = layer_norm(DN_ALPHA * h + mixed, ln1_g[l], ln1_b[l])
        ffn = hier_moe(x, w_group[l], b_group[l], w_expert[l], b_expert[l], w_gate_up[l], w_down[l])
        x = layer_norm(DN_ALPHA * x + ffn, ln2_g[l], ln2_b[l])
    return x


DEPTH_2 = 2

FOX_HEADS = 8
FOX_HEAD_DIM = 64
DIFF_HEADS = 4
DIFF_HEAD_DIM = 64
DIFF_V_DIM = 2 * DIFF_HEAD_DIM
FOX_WIDTH = FOX_HEADS * FOX_HEAD_DIM
DIFF_WIDTH = DIFF_HEADS * DIFF_V_DIM
MIX_WIDTH = FOX_WIDTH + DIFF_WIDTH
D_FF = 2816
Q_BLOCK = 128
ROPE_THETA = 10000.0
FFN_RES_WEIGHT = 0.5
IN_SPLITS = [FOX_WIDTH, FOX_WIDTH, FOX_WIDTH, FOX_HEADS,
             2 * DIFF_HEADS * DIFF_HEAD_DIM, 2 * DIFF_HEADS * DIFF_HEAD_DIM, DIFF_WIDTH]
IN_COLS_2 = int(sum(IN_SPLITS))
IN_OFFSETS = [int(v) for v in np.cumsum(IN_SPLITS)[:-1]]


def _rmsnorm(x, gain):
    x32 = x.astype(jnp.float32)
    y = x32 * lax.rsqrt(jnp.mean(x32 * x32, axis=-1, keepdims=True) + NORM_EPS)
    return (y * gain.astype(jnp.float32)).astype(x.dtype)

def _swiglu(h, w_gate_up, w_down):
    g, u = jnp.split(h @ w_gate_up, 2, axis=-1)
    return (jax.nn.silu(g) * u) @ w_down

def _rope_tables(seq, dim):
    inv_freq = 1.0 / (ROPE_THETA ** (jnp.arange(0, dim, 2, dtype=jnp.float32) / dim))
    pos = jnp.arange(seq, dtype=jnp.float32)
    freqs = pos[:, None] * inv_freq[None, :]
    emb = jnp.concatenate([freqs, freqs], axis=-1)
    return jnp.cos(emb), jnp.sin(emb)

def _apply_rope(t, cos, sin):
    t32 = t.astype(jnp.float32)
    t1, t2 = jnp.split(t32, 2, axis=-1)
    rot = jnp.concatenate([-t2, t1], axis=-1)
    return (t32 * cos + rot * sin).astype(t.dtype)

def _causal_block_attention(q_f, k_f, v_f, cum_f, q_d, k_d, v_d, lam):
    B, Hf, S, Df = q_f.shape
    Hd, Dh = q_d.shape[1], q_d.shape[-1]
    Dv = v_d.shape[-1]
    nb = S // Q_BLOCK
    qf_blk = jnp.moveaxis(q_f.reshape(B, Hf, nb, Q_BLOCK, Df), 2, 0)
    cf_blk = jnp.moveaxis(cum_f.reshape(B, Hf, nb, Q_BLOCK), 2, 0)
    qd_blk = jnp.moveaxis(q_d.reshape(B, Hd, 2, nb, Q_BLOCK, Dh), 3, 0)
    k_pos = jnp.arange(S)
    scale_f = Df ** -0.5
    scale_d = Dh ** -0.5

    def one_block(args):
        qf, cf, qd, blk = args
        q_pos = blk * Q_BLOCK + jnp.arange(Q_BLOCK)
        causal = k_pos[None, :] <= q_pos[:, None]
        s_f = jnp.einsum('bhqd,bhkd->bhqk', qf, k_f).astype(jnp.float32) * scale_f
        s_f = s_f + cf[..., :, None] - cum_f[..., None, :]
        s_f = jnp.where(causal, s_f, -jnp.inf)
        p_f = jax.nn.softmax(s_f, axis=-1)
        o_f = jnp.einsum('bhqk,bhkd->bhqd', p_f.astype(v_f.dtype), v_f)
        s_d = jnp.einsum('bhcqd,bhckd->bhcqk', qd, k_d).astype(jnp.float32) * scale_d
        s_d = jnp.where(causal, s_d, -jnp.inf)
        p_d = jax.nn.softmax(s_d, axis=-1)
        a_d = p_d[:, :, 0] - lam * p_d[:, :, 1]
        o_d = jnp.einsum('bhqk,bhkd->bhqd', a_d.astype(v_d.dtype), v_d)
        return o_f, o_d

    o_f, o_d = lax.map(one_block, (qf_blk, cf_blk, qd_blk, jnp.arange(nb)))
    o_f = jnp.moveaxis(o_f, 0, 2).reshape(B, Hf, S, Df)
    o_d = jnp.moveaxis(o_d, 0, 2).reshape(B, Hd, S, Dv)
    return o_f, o_d

def _hybrid_mixer(h, w_in, forget_bias, lq1, lk1, lq2, lk2, subln, w_out, lambda_init):
    B, S, _ = h.shape
    proj = h @ w_in
    fq, fk, fv, ff, dq, dk, dv = jnp.split(proj, IN_OFFSETS, axis=-1)
    to_heads_f = lambda t: t.reshape(B, S, FOX_HEADS, FOX_HEAD_DIM).transpose(0, 2, 1, 3)
    q_f, k_f, v_f = to_heads_f(fq), to_heads_f(fk), to_heads_f(fv)
    log_f = jax.nn.log_sigmoid((ff + forget_bias).astype(jnp.float32))
    cum_f = jnp.cumsum(log_f.transpose(0, 2, 1), axis=-1)
    to_heads_d = lambda t: t.reshape(B, S, DIFF_HEADS, 2, DIFF_HEAD_DIM).transpose(0, 2, 3, 1, 4)
    cos, sin = _rope_tables(S, DIFF_HEAD_DIM)
    q_d = _apply_rope(to_heads_d(dq), cos, sin)
    k_d = _apply_rope(to_heads_d(dk), cos, sin)
    v_d = dv.reshape(B, S, DIFF_HEADS, DIFF_V_DIM).transpose(0, 2, 1, 3)
    lam = (jnp.exp(jnp.sum(lq1.astype(jnp.float32) * lk1.astype(jnp.float32)))
           - jnp.exp(jnp.sum(lq2.astype(jnp.float32) * lk2.astype(jnp.float32)))
           + lambda_init)
    o_f, o_d = _causal_block_attention(q_f, k_f, v_f, cum_f, q_d, k_d, v_d, lam)
    o_d = _rmsnorm(o_d, subln) * (1.0 - lambda_init)
    o_f = o_f.transpose(0, 2, 1, 3).reshape(B, S, FOX_WIDTH)
    o_d = o_d.transpose(0, 2, 1, 3).reshape(B, S, DIFF_WIDTH)
    return jnp.concatenate([o_f, o_d], axis=-1) @ w_out

def second_inputs(seed: int = 0) -> dict:
    key = jax.random.key(seed)
    ks = jax.random.split(key, 20)
    nrm = lambda k, shape, fan_in: jax.random.normal(k, shape, jnp.float32) * fan_in ** -0.5
    gain = lambda k, shape: 1.0 + 0.02 * jax.random.normal(k, shape, jnp.float32)
    return {
        "x": jax.random.normal(ks[0], (BATCH, SEQ, D_MODEL), jnp.float32),
        "ffn1_norm": gain(ks[1], (DEPTH_2, D_MODEL)),
        "ffn1_w_gate_up": nrm(ks[2], (DEPTH_2, D_MODEL, 2 * D_FF), D_MODEL),
        "ffn1_w_down": nrm(ks[3], (DEPTH_2, D_FF, D_MODEL), D_FF),
        "mix_norm": gain(ks[4], (DEPTH_2, D_MODEL)),
        "w_in": nrm(ks[5], (DEPTH_2, D_MODEL, IN_COLS_2), D_MODEL),
        "forget_bias": jax.random.uniform(ks[6], (DEPTH_2, FOX_HEADS), jnp.float32, 1.0, 4.0),
        "lambda_q1": 0.1 * jax.random.normal(ks[7], (DEPTH_2, DIFF_HEAD_DIM), jnp.float32),
        "lambda_k1": 0.1 * jax.random.normal(ks[8], (DEPTH_2, DIFF_HEAD_DIM), jnp.float32),
        "lambda_q2": 0.1 * jax.random.normal(ks[9], (DEPTH_2, DIFF_HEAD_DIM), jnp.float32),
        "lambda_k2": 0.1 * jax.random.normal(ks[10], (DEPTH_2, DIFF_HEAD_DIM), jnp.float32),
        "diff_subln": gain(ks[11], (DEPTH_2, DIFF_V_DIM)),
        "w_out": nrm(ks[12], (DEPTH_2, MIX_WIDTH, D_MODEL), MIX_WIDTH),
        "ffn2_norm": gain(ks[13], (DEPTH_2, D_MODEL)),
        "ffn2_w_gate_up": nrm(ks[14], (DEPTH_2, D_MODEL, 2 * D_FF), D_MODEL),
        "ffn2_w_down": nrm(ks[15], (DEPTH_2, D_FF, D_MODEL), D_FF),
        "final_norm": gain(ks[16], (D_MODEL,)),
    }

def second_block(x, ffn1_norm, ffn1_w_gate_up, ffn1_w_down, mix_norm, w_in, forget_bias,
              lambda_q1, lambda_k1, lambda_q2, lambda_k2, diff_subln, w_out,
              ffn2_norm, ffn2_w_gate_up, ffn2_w_down, final_norm):
    for layer in range(DEPTH_2):
        lambda_init = 0.8 - 0.6 * math.exp(-0.3 * layer)
        x = x + FFN_RES_WEIGHT * _swiglu(_rmsnorm(x, ffn1_norm[layer]),
                                         ffn1_w_gate_up[layer], ffn1_w_down[layer])
        x = x + _hybrid_mixer(_rmsnorm(x, mix_norm[layer]), w_in[layer], forget_bias[layer],
                              lambda_q1[layer], lambda_k1[layer], lambda_q2[layer],
                              lambda_k2[layer], diff_subln[layer], w_out[layer], lambda_init)
        x = x + FFN_RES_WEIGHT * _swiglu(_rmsnorm(x, ffn2_norm[layer]),
                                         ffn2_w_gate_up[layer], ffn2_w_down[layer])
    return _rmsnorm(x, final_norm)


def setup_inputs(seed=0):
    out = dict(first_inputs(seed))
    for name, value in second_inputs(seed + 1).items():
        if name != "x":
            out[name + "_2"] = value
    return out


def reference(
    x, w_in, b_in, lb_logits, hg_norm_g, rel_bias, w_proj_a, w_proj_b, w_out, ln1_g, ln1_b,
    w_group, b_group, w_expert, b_expert, w_gate_up, w_down, ln2_g, ln2_b, ffn1_norm_2,
    ffn1_w_gate_up_2, ffn1_w_down_2, mix_norm_2, w_in_2, forget_bias_2, lambda_q1_2,
    lambda_k1_2, lambda_q2_2, lambda_k2_2, diff_subln_2, w_out_2, ffn2_norm_2, ffn2_w_gate_up_2,
    ffn2_w_down_2, final_norm_2,
):
    x = first_block(
        x, w_in, b_in, lb_logits, hg_norm_g, rel_bias, w_proj_a, w_proj_b, w_out, ln1_g, ln1_b,
        w_group, b_group, w_expert, b_expert, w_gate_up, w_down, ln2_g, ln2_b,
    )
    return second_block(
        x, ffn1_norm_2, ffn1_w_gate_up_2, ffn1_w_down_2, mix_norm_2, w_in_2, forget_bias_2,
        lambda_q1_2, lambda_k1_2, lambda_q2_2, lambda_k2_2, diff_subln_2, w_out_2, ffn2_norm_2,
        ffn2_w_gate_up_2, ffn2_w_down_2, final_norm_2,
    )


_drawn_inputs = setup_inputs


def setup_inputs(seed=0):
    import zlib

    import numpy as np

    out = dict(_drawn_inputs(seed))
    spreads = {}
    factors = {'lb_logits': 3.875,
     'hg_norm_g': 2.798,
     'rel_bias': 3.114,
     'b_group': 4.058,
     'b_expert': 4.35,
     'ffn1_norm_2': 4.287,
     'lambda_q1_2': 4.528,
     'diff_subln_2': 17.005,
     'ffn2_norm_2': 5.815,
     'final_norm_2': 7.493,
     'mix_norm_2': 2.973,
     'lambda_q2_2': 3.714,
     'lambda_k2_2': 3.305}
    for name, (base, spread) in spreads.items():
        noise = np.random.default_rng([zlib.crc32(name.encode()), seed]).standard_normal(out[name].shape)
        drawn = base * np.exp(spread * noise) if base else spread * noise
        out[name] = __import__('jax').numpy.asarray(drawn.astype(out[name].dtype))
    for name, factor in factors.items():
        out[name] = (out[name] * factor).astype(out[name].dtype)
    return out
```

```python
import math
from contextlib import ExitStack

import numpy as np

import concourse.bass as bass
from concourse import mybir

F32 = mybir.dt.float32
F32R = mybir.dt.float32r
I32 = mybir.dt.int32
ALU = mybir.AluOpType
ACT = mybir.ActivationFunctionType
AX = mybir.AxisListType

P = 128
T = 256
TT = T // P
D = 1024
KB = D // P
HG_HEADS = 4
SUB = 16
NSUB = T // SUB
MB_HEADS = 8
DH = 64
BUCKETS = 32
MAX_DIST = 128
GROUPS = 4
PER_GROUP = 8
EXPERTS = GROUPS * PER_GROUP
ROUTED = GROUPS + EXPERTS
TOP_K = 2
LAYERS = 2
D_FF = 2816
CHUNKS = D_FF // P
EPS = 1e-5
ALPHA = 2.0 ** 0.25
NEG = -1e30

PER_SLOT = 24
SLOT = PER_SLOT * P
RING = 8
RAW = (6, 7, 0, 1)
PART_A = 16
LAG = 2
VCOLS = 256
V_SLOTS = 4
T_BLOCKS = 36
FIRST_SLOTS = 16 + 6
EXPERT_SLOTS = 4
MOE_SLOTS = EXPERTS * EXPERT_SLOTS
MIX_AT = CHUNKS
FFN2_AT = MIX_AT + V_SLOTS + 8
LAYER_SLOTS = FFN2_AT + CHUNKS
LAYER_AT = FIRST_SLOTS + MOE_SLOTS
WIN = 128
ASSIGNED = T * TOP_K
ROUTER_AT = 8 * P
FIRST_UNITS = 22
LAYER_UNITS = 12
LOCAL = T + P

CONSTS = {"ident": P, "ones": P, "tri": P, "tri_strict": P, "rot": P, "band": SUB * SUB,
          "blk": P // SUB, "rev_group": GROUPS, "rev_expert": EXPERTS, "bucket": T,
          "lam_init": 2 * LAYERS}
LATE = {"cos": T, "sin": T, "causal": TT * T, "forget": LAYERS * KB * 8}
PARAMS = {"b_in": T_BLOCKS, "lb": 8, "hg_g": 4, "ln1_g": 8, "ln1_b": 8, "ln2_g": 8, "ln2_b": 8,
          "rel": 8, "final": 8, "layers": LAYERS * 29}
LAYER_PARAMS = {"ffn1": 8, "mix": 8, "ffn2": 8, "subln": 1, "lam": 4}
ROWS = {"b_router": ROUTED, "forget": LAYERS * 8}


def offsets(widths):
    at, out = 0, {}
    for name, width in widths.items():
        out[name] = (at, width)
        at += width
    return out, at


def attention_units(kind):
    if kind == "moba":
        return [("m", h) for h in range(8)], [(h, ("m", h)) for h in range(8)]
    scores = [("f", h) for h in range(8)] + [("d", c) for c in range(8)]
    return scores, [(h, ("f", h)) for h in range(8)] + [(9 + 2 * h, ("d", h)) for h in range(4)]


def projection_units():
    return ([("t", b) for b in range(0, 12, 2)] + [("v", v) for v in range(V_SLOTS)]
            + [("t", b) for b in range(12, T_BLOCKS, 2)])


class Chain:

    def __init__(self, eng, sem):
        self.eng, self.sem, self.n = eng, sem, 0

    def __call__(self, instruction):
        instruction.then_inc(self.sem, 1)
        self.n += 1
        self.eng.wait_ge(self.sem, self.n)

    def mark(self, instruction):
        instruction.then_inc(self.sem, 1)
        self.n += 1

    def wait(self):
        self.eng.wait_ge(self.sem, self.n)

    def restart(self):
        if self.n:
            self.eng.wait_ge(self.sem, self.n)
            self.eng.sem_clear(self.sem)
            self.n = 0


def program(nc, x_in, first_w, moe_w, layer_w, consts_in, late_in, iota_in, params_in, rows_in, b_v_in, out):
    ctx = ExitStack()
    with ctx:
        def sb(name, shape, dt=F32):
            return ctx.enter_context(nc.sbuf_tensor(name, shape, dt))

        def overlaid(name, shape, before, parts, after):
            with nc.sbuf_tensor(name, shape, F32) as first:
                pass
            sb(f"{name}_before", [P, before])
            later = [sb(part, [P, *s], F32R) for part, s in parts.items()]
            if after:
                sb(f"{name}_after", [P, after])
            return first, *later

        sems = {}

        def S(name):
            if name not in sems:
                sems[name] = ctx.enter_context(nc.semaphore(name))
            return sems[name]

        c_at, c_n = offsets(CONSTS)
        late_at, late_n = offsets(LATE)
        p_at, p_n = offsets(PARAMS)
        l_at, l_n = offsets(LAYER_PARAMS)
        r_at, r_n = offsets(ROWS)
        consts = sb("consts", [P, c_n])
        params = sb("params", [P, p_n])
        cur = sb("cur", [P, l_n + 2])
        rows = sb("rows", [1, r_n])
        ring, w_hi, w_lo = overlaid("ring", [P, RING, SLOT], 2 * SLOT,
                                    {"w_hi": (2, SLOT), "w_lo": (2, SLOT)}, 2 * SLOT)
        x_t = sb("x_t", [P, KB, T])
        h_t = sb("h_t", [P, KB, T])
        sq = sb("sq", [P, KB, T])
        stat = sb("stat", [P, 4, T])
        vtok = sb("vtok", [P, TT, D])
        probs = sb("probs", [P, 4, TT, T])
        probs_t = sb("probs_t", [P, 2, TT, T])
        small = sb("small", [P, 4, 4, TT])
        meta = sb("meta", [1, 3 * EXPERTS], I32)
        lbs = sb("lbs", [P, 24])
        negb = sb("negb", [P, 4])
        lams = sb("lams", [P, 8])
        ffs = sb("ffs", [P, 6, TT, 8])
        band = sb("band", [P, 8, SUB])
        decays = sb("decays", [P, 2, 4 * NSUB])

        AREA = 14336
        SPLIT = 2 * (KB + 2) * T
        area, h_hi, h_lo, hid_hi, hid_lo = overlaid(
            "area", [P, AREA], AREA - SPLIT,
            {"h_hi": (KB, T), "h_lo": (KB, T), "hid_hi": (2, T), "hid_lo": (2, T)}, 0)

        def carve(sizes, limit=AREA):
            at, got = 0, {}
            for name, shape in sizes.items():
                n = math.prod(shape)
                v = area[:, at:at + n]
                if len(shape) > 1:
                    names = "abcd"[:len(shape)]
                    v = v.rearrange(f"p ({' '.join(names)}) -> p {' '.join(names)}", **dict(zip(names, shape)))
                got[name] = v
                at += n
            assert at <= limit, at
            return got

        one = carve({"q": (4, T), "f": (4, T), "g": (4, T), "k": (4, T), "mq": (4, T), "mk": (4, T),
                     "gates": (16, T), "grow": (4, T), "bias": (MB_HEADS, LOCAL)})
        q_hg, f_hg, g_hg, k_hg = one["q"], one["f"], one["g"], one["k"]
        mq, mk, gates, grow, bias = one["mq"], one["mk"], one["gates"], one["grow"], one["bias"]
        b_v = gates[0:1, 0:4, :].rearrange("p a t -> p (a t)")
        band_p = probs[:, :, :, :].rearrange("p (r c) j t -> p r (c j) t", r=2)
        kdec = sq[:, :, :].rearrange("p (r h) t -> p r h t", r=2)
        hg_scores = h_t[:, :, :].rearrange("p (h j) t -> p h j t", j=TT)
        wide = h_t[:, :, :].rearrange("p n (d t) -> p n d t", d=SUB)
        bias_row = probs_t[0:8, 0, :, :].rearrange("p a t -> p (a t)")
        two = carve({"xs": (KB, ASSIGNED + WIN), "ys": (KB, ASSIGNED + WIN), "mixw_t": (ASSIGNED // P, T),
                     "sg": (4 * WIN,), "hid": (4, WIN)})
        xs, ys, mixw_t = two["xs"], two["ys"], two["mixw_t"]
        before_ys = ys.rearrange("p k n -> p (k n)")
        pick, mixw, mixw_2 = (before_ys[:, TT * ASSIGNED * i:TT * ASSIGNED * (i + 1)]
                              .rearrange("p (j n) -> p j n", j=TT) for i in range(3))
        iota = before_ys[:, 3 * TT * ASSIGNED:3 * TT * ASSIGNED + ASSIGNED]
        ys_tok = area[:, 0:ASSIGNED // P * D].rearrange("p (i n) -> p i n", i=ASSIGNED // P)
        routing = probs[:, 0:2, :, :].rearrange("p r a t -> p (r a t)")
        counts_t = probs[0:EXPERTS, 2, :, :].rearrange("p a t -> p (a t)")
        three = carve({"qk": (16, T), "rot": (2, 2, T), "od": (4, T), "ncum": (T,), "sg": (2, T),
                       "hid": (2, T), "late": (late_n,)}, AREA - SPLIT)
        qk, od, ncum, rotated = three["qk"], three["od"], three["ncum"], three["rot"]
        scratch = nc.dram_tensor("bias_rows_dram", [8, 2 * T], F32, kind="Internal").ap()
        copies = nc.dram_tensor("bias_copies_dram", [P, MB_HEADS * 2 * T], F32, kind="Internal").ap()
        ps = [ctx.enter_context(nc.psum_tensor(f"bank{i}", [P, 512], F32)) for i in range(8)]
        ring_full = [S(f"ring_full{i}") for i in range(RING)]

        def const(name, parts=P):
            at, n = c_at[name]
            return consts[0:parts, at:at + n]

        def late(name):
            at, n = late_at[name]
            return three["late"][:, at:at + n]

        def param(name, i, n=1, parts=P):
            at = p_at[name][0] + i
            return params[0:parts, at:at + n]

        def row(name, i, n):
            at = r_at[name][0] + i
            return rows[0:1, at:at + n]

        def gain(name, b):
            at = l_at[name][0] + b
            return cur[:, at:at + 1]

        def halves(bank):
            return ps[bank][:, :].rearrange("p (a t) -> p a t", a=2)

        def settled(eng):
            eng.sem_inc(S("waits_passed"), 1)

        layer_full = [S(f"layer_full{i}") for i in range(len(RAW))]
        ones, ident = const("ones"), const("ident")
        block = ctx.enter_context(nc.Block())

        @block.sync
        def _(sp):
            def fill(n, src):
                sp.dma_start(ring[:, n % RING, :], src).then_inc(ring_full[n % RING], 16)

            def slot_of(w, at):
                return w[bass.ds(at, 1)].rearrange("a p n -> (a p) n")

            sp.dma_start(x_t[:], x_in).then_inc(S("x_loaded"), 16)
            for n in range(FIRST_SLOTS + 2 * EXPERT_SLOTS):
                if n >= RING and n < FIRST_SLOTS + RING - LAG:
                    sp.wait_ge(S("slot_used"), n - RING + LAG + 1)
                elif n >= RING:
                    sp.wait_ge(S("logits_done"), 1)
                fill(n, first_w[n] if n < FIRST_SLOTS else moe_w[n - FIRST_SLOTS])
            sp.wait_ge(S("meta_ready"), 1)
            with sp.Fori(0, EXPERTS // 2 - 1) as pair:
                for half in range(2):
                    before = sp.value_load(meta[0:1, bass.ds(2 * EXPERTS + 2 * pair + half + 1, 1)],
                                           min_val=1, max_val=EXPERTS + ASSIGNED // WIN)
                    for i in range(EXPERT_SLOTS):
                        if i == 0:
                            sp.wait_ge(S("down_done"), before)
                        fill(FIRST_SLOTS + EXPERT_SLOTS * half + i,
                             slot_of(moe_w, 2 * EXPERT_SLOTS * (pair + 1) + EXPERT_SLOTS * half + i))
            before = sp.value_load(meta[0:1, 3 * EXPERTS - 1:3 * EXPERTS], min_val=1,
                                   max_val=EXPERTS + ASSIGNED // WIN)
            sp.wait_ge(S("down_done"), before)
            settled(sp)
            for i, place in enumerate(RAW):
                sp.dma_start(ring[:, place, :], layer_w[i]).then_inc(layer_full[i], 16)
            with sp.Fori(0, LAYERS * LAYER_SLOTS // len(RAW) - 1) as g:
                for i, place in enumerate(RAW):
                    sp.wait_ge(S("lo_ready"), 2 * len(RAW) * g + 2 * i + 2)
                    sp.dma_start(ring[:, place, :], slot_of(layer_w, len(RAW) * (g + 1) + i))\
                        .then_inc(layer_full[i], 16)
            sp.wait_ge(S("h_made"), KB * (3 * LAYERS + 1))
            sp.dma_start(out, h_t[:]).then_inc(S("stored"), 16)
            sp.wait_ge(S("stored"), 16)

        @block.gpsimd
        def _(pool):
            own = Chain(pool, S("pool_own"))
            pool.dma_start(consts[:], consts_in).then_inc(S("consts_loaded"), 16)
            pool.dma_start(params[:], params_in).then_inc(S("params_loaded"), 16)
            pool.dma_start(rows[:], rows_in).then_inc(S("rows_loaded"), 16)
            pool.dma_start(b_v, b_v_in).then_inc(S("b_v_loaded"), 16)
            pool.memset(probs[:], 0.0).then_inc(S("band_p_zero"), 1)
            pool.memset(sq[:], 0.0).then_inc(S("kdec_zero"), 1)
            own(pool.memset(bias_row[:, T:2 * T], NEG))
            pool.wait_ge(S("bias_row_ready"), 1)
            pool.dma_start(scratch, bias_row).then_inc(S("bias_stored"), 16)
            pool.wait_ge(S("bias_stored"), 16)
            rows_of = MB_HEADS * 2 * T
            pool.dma_start(copies, bass.AP(tensor=scratch.tensor, offset=0, ap=[[0, P], [1, rows_of]]))\
                .then_inc(S("bias_copied"), 16)
            pool.wait_ge(S("bias_copied"), 16)
            src = bass.AP(tensor=copies.tensor, offset=P - 1, ap=[[rows_of - 1, P], [2 * T, MB_HEADS], [1, LOCAL]])
            pool.dma_start(bias, src).then_inc(S("bias_loaded"), 16)

            def attention(kind, s0, o0):
                scores, outs = attention_units(kind)
                ends = [last for last, _ in outs]
                for s, (what, c) in enumerate(scores):
                    pool.wait_ge(S("recip_ready"), s0 + s + 1)
                    settled(pool)
                    for j in range(TT):
                        p = probs[:, s % 4, j, :]
                        n = pool.tensor_scalar(p, p, small[:, s % 4, 3, j:j + 1], None, ALU.mult)
                    if what != "d":
                        n.then_inc(S("probs_ready"), 1)
                    elif c % 2 == 0:
                        own.mark(n)
                    else:
                        own(n)
                        a, b = probs[:, s % 4, :, :], probs[:, (s - 1) % 4, :, :]
                        pool.tensor_tensor(a, a, b, ALU.add).then_inc(S("probs_ready"), 1)

            attention("moba", 0, 0)
            pool.wait_ge(S("router_in"), 1)
            pool.dma_start(iota, iota_in).then_inc(S("iota_loaded"), 16)
            pool.memset(xs[:, :, ASSIGNED:], 0.0).then_inc(S("xs_zero"), 1)
            pool.wait_ge(S("x_updates"), 2)
            pool.dma_start(three["late"], late_in).then_inc(S("late_loaded"), 16)
            own.restart()
            with pool.Fori(0, LAYERS) as layer:
                attention("layer", 8 + 16 * layer, 8 + 12 * layer)
                own.restart()

        @block.tensor
        def _(pe):
            def arrived(n, more=0):
                pe.wait_ge(ring_full[n % RING], 16 * (n // RING + 1) + 16 * more)
                return n % RING

            def sub_product(out_ap, n0, i, moving, **flags):
                n = n0 + i // PER_SLOT
                if i % PER_SLOT == 0:
                    arrived(n)
                at = i % PER_SLOT * P
                m = pe.matmul(out_ap, ring[:, n % RING, at:at + P], moving, **flags)
                if i % PER_SLOT == 0:
                    m.then_inc(S("slot_used"), 1)
                return m

            def half(bank, i, parts=P):
                return ps[bank][0:parts, i * T:(i + 1) * T]

            def column_sums(bank, src):
                for b in range(KB):
                    last = pe.matmul(half(bank, 0), ones, src[:, b, :], start=b == 0, stop=b == KB - 1)
                last.then_inc(S("sum_ready"), 1)

            def attention(kind, s0, o0):
                scores, outs = attention_units(kind)

                def score(s):
                    what, h = scores[s]
                    if s >= 2:
                        pe.wait_ge(S("score_read"), s0 + s - 1)
                    po = DH * (h % 2)
                    if what == "m":
                        q, k = mq[po:po + DH, h // 2, :], mk[po:po + DH, h // 2, :]
                    else:
                        at = h // 2 + (8 if what == "d" else 0)
                        q, k = qk[po:po + DH, at, :], qk[po:po + DH, at + 4, :]
                    for j in range(TT):
                        last = pe.matmul(half(s % 2, j), q[:, j * P:(j + 1) * P], k, start=True, stop=what != "f")
                        if what == "f":
                            last = pe.matmul(half(s % 2, j), ident[0:8, h:h + 1].to_broadcast([8, P]), ncum[0:8, :],
                                             start=False, stop=True)
                    last.then_inc(S("score_done"), 1)

                def turn(o):
                    s = outs[o][0]
                    pe.wait_ge(S("probs_ready"), o0 + o + 1)
                    if o >= 2:
                        pe.wait_ge(S("turned_copied"), o0 + o - 1)
                    for i in range(TT):
                        for j in range(TT):
                            last = pe.transpose(ps[2 + o % 2][:, i * T + j * P:i * T + (j + 1) * P],
                                                probs[:, s % 4, j, i * P:(i + 1) * P], ident)
                    last.then_inc(S("turned"), 1)

                def values(o):
                    what, h = outs[o][1]
                    pe.wait_ge(S("turned_copied"), o0 + o + 1)
                    if o >= 2:
                        pe.wait_ge(S("o_copied"), o0 + o - 1)
                    if what == "d":
                        at, w, po = 512 + h * P, P, 0
                    else:
                        at, w, po = (512 if what == "m" else 0) + h * DH, DH, DH * (h % 2)
                    for i in range(TT):
                        last = pe.matmul(ps[4 + o % 2][po:po + w, 0:T], vtok[:, i, at:at + w],
                                         probs_t[:, o % 2, i, :], start=i == 0, stop=i == TT - 1)
                    last.then_inc(S("o_ready"), 1)

                for s in range(len(scores) + 2):
                    if s < len(scores):
                        score(s)
                    for o, (end, _) in enumerate(outs):
                        if end == s - 1:
                            turn(o)
                        if end == s - 2:
                            values(o)

            def out_product(n0, first, src):
                for j in range(KB):
                    for k in range(KB):
                        last = sub_product(half(4 + j // 2, j % 2), n0, first + j * KB + k, src[:, k, :],
                                           start=k == 0, stop=k == KB - 1)
                last.then_inc(S("wide_done"), 1)

            for name in ("consts_loaded", "params_loaded", "rows_loaded", "b_v_loaded", "x_loaded"):
                pe.wait_ge(S(name), 16)
            pe.matmul(half(5, 0, 8), param("rel", 0, 8, BUCKETS), const("bucket", BUCKETS),
                      start=True, stop=True).then_inc(S("bias_row_done"), 1)

            def diagonal(d):
                pe.wait_ge(S("band_p_ready"), d + 1)
                for h in range(HG_HEADS):
                    for j in range(TT):
                        c = (h * TT + j) * SUB + d
                        last = pe.matmul(ps[4][:, c:c + 1], band_p[:, d % 2, h, j * P:(j + 1) * P], ones[:, 0:1],
                                         start=True, stop=True)
                last.then_inc(S("band_done"), 1)

            def earlier(i):
                if i == 1:
                    pe.wait_ge(S("band_copied"), 1)
                    pe.wait_ge(S("bias_row_ready"), 1)
                pe.wait_ge(S("kdec_ready"), i)
                for h in range(HG_HEADS):
                    for j in range(TT if i > NSUB // TT else 1):
                        last = pe.matmul(ps[4 + h][:, j * T + i * SUB:j * T + (i + 1) * SUB],
                                         kdec[:, i % 2, h, j * P:(j + 1) * P], q_hg[:, h, i * SUB:(i + 1) * SUB],
                                         start=True, stop=True)
                last.then_inc(S("earlier_done"), 1)

            between = [lambda d=d: diagonal(d) for d in range(SUB)] + [lambda i=i: earlier(i) for i in range(1, NSUB)]
            for u, (what, b) in enumerate(projection_units()):
                if u >= 4:
                    pe.wait_ge(S("proj_read"), u - 3)
                if what == "t":
                    for side in range(2):
                        first = (b + side) * KB + (V_SLOTS * PER_SLOT if b >= 12 else 0)
                        for k in range(KB):
                            last = sub_product(half(u % 4, side), 0, first + k, x_t[:, k, :],
                                               start=k == 0, stop=k == KB - 1)
                else:
                    slot = arrived(4 + b)
                    for j in range(TT):
                        for k in range(KB):
                            m = pe.matmul(half(u % 4, j), x_t[:, k, j * P:(j + 1) * P],
                                          ring[:, slot, k * VCOLS:(k + 1) * VCOLS], start=k == 0, stop=False)
                            if j == 0 and k == 0:
                                m.then_inc(S("slot_used"), 1)
                        last = pe.matmul(half(u % 4, j), ones[0:1, :], b_v[:, b * VCOLS:(b + 1) * VCOLS],
                                         start=False, stop=True)
                last.then_inc(S("proj_done"), 1)
                if u >= 6:
                    for _ in range(2):
                        if between:
                            between.pop(0)()
            for step in between:
                step()

            pe.wait_ge(S("hg_scores_ready"), 1)
            for h in range(HG_HEADS):
                for j in range(TT):
                    last = pe.matmul(half(6 + h // 2, h % 2), vtok[:, j, h * P:(h + 1) * P], hg_scores[:, h, j, :],
                                     start=j == 0, stop=j == TT - 1)
            last.then_inc(S("hg_o_ready"), 1)
            pe.wait_ge(S("hg_sq_ready"), 1)
            for h in range(HG_HEADS):
                last = pe.matmul(half(6 + h // 2, h % 2), ones, sq[:, h, :], start=True, stop=True)
            last.then_inc(S("hg_sum_ready"), 1)

            pe.wait_ge(S("proj_read"), FIRST_UNITS)
            attention("moba", 0, 0)

            pe.wait_ge(S("o_copied"), MB_HEADS)
            for j in range(KB):
                if j >= 4:
                    pe.wait_ge(S("mixed_ready"), j - 3)
                for side in range(2):
                    for k in range(4):
                        last = sub_product(half(j % 4, side), 16, j * KB + side * 4 + k, h_t[:, side * 4 + k, :],
                                           start=k == 0, stop=k == 3)
                last.then_inc(S("ab_done"), 1)
            pe.wait_ge(S("mixed_ready"), KB)
            out_product(16, KB * KB, sq)
            pe.wait_ge(S("x_updates"), 1)
            column_sums(0, x_t)
            pe.wait_ge(S("sq_ready"), 1)
            column_sums(1, sq)
            pe.wait_ge(S("router_in"), 1)

            for j in range(TT):
                out_ap = ps[2][:, j * ROUTED:(j + 1) * ROUTED]
                for k in range(KB):
                    at = ROUTER_AT + k * ROUTED
                    pe.matmul(out_ap, x_t[:, k, j * P:(j + 1) * P], ring[:, (FIRST_SLOTS - 1) % RING, at:at + ROUTED],
                              start=k == 0, stop=False)
                last = pe.matmul(out_ap, ones[0:1, :], row("b_router", 0, ROUTED), start=False, stop=True)
            last.then_inc(S("logits_done"), 1)
            for j in range(TT):
                for k in range(KB):
                    last = pe.transpose(ps[4 + 2 * j + k // 4][:, k % 4 * P:(k % 4 + 1) * P],
                                        x_t[:, k, j * P:(j + 1) * P], ident)
            last.then_inc(S("x_tok_done"), 1)
            pe.wait_ge(S("assigned_ready"), 1)
            assigned = routing[:, 0:TT * EXPERTS].rearrange("p (j e) -> p j e", j=TT)
            strict = const("tri_strict")
            pe.matmul(ps[3][:, 0:EXPERTS], strict, assigned[:, 0, :], start=True, stop=True)
            pe.matmul(ps[3][:, EXPERTS:2 * EXPERTS], ones, assigned[:, 0, :], start=True, stop=False)
            pe.matmul(ps[3][:, EXPERTS:2 * EXPERTS], strict, assigned[:, 1, :], start=False, stop=True)
            pe.matmul(ps[3][0:EXPERTS, P:2 * P], assigned[:, 0, :], ones, start=True, stop=False)
            pe.matmul(ps[3][0:EXPERTS, P:2 * P], assigned[:, 1, :], ones, start=False, stop=True)\
                .then_inc(S("counts_done"), 1)
            pe.wait_ge(S("counts_ready"), 1)
            few = strict[0:EXPERTS, 0:EXPERTS]
            pe.matmul(ps[2][:, 128:128 + EXPERTS], counts_t[:, 0:P], few, start=True, stop=True)
            pe.matmul(ps[2][:, 160:160 + EXPERTS], counts_t[:, P:2 * P], ident[0:EXPERTS, 0:EXPERTS],
                      start=True, stop=True)
            pe.matmul(ps[2][:, 192:192 + EXPERTS], counts_t[:, P:2 * P], few, start=True, stop=True)\
                .then_inc(S("starts_done"), 1)
            pe.wait_ge(S("x_tok_ready"), 1)
            pe.wait_ge(S("pick_ready"), 1)
            for k in range(KB):
                if k >= 4:
                    pe.wait_ge(S("xs_ready"), k - 3)
                for j in range(TT):
                    last = pe.matmul(ps[4 + k % 4][:, :], vtok[:, j, k * P:(k + 1) * P], pick[:, j, :],
                                     start=j == 0, stop=j == TT - 1)
                last.then_inc(S("gathered"), 1)
            pe.wait_ge(S("mixw_ready"), 1)
            for i in range(ASSIGNED // P):
                for j in range(TT):
                    last = pe.transpose(ps[i // 2][:, i % 2 * T + j * P:i % 2 * T + (j + 1) * P],
                                        mixw[:, j, i * P:(i + 1) * P], ident)
            last.then_inc(S("mixw_turned"), 1)
            pe.wait_ge(S("xs_ready"), KB)
            pe.wait_ge(S("xs_zero"), 1)
            pe.wait_ge(S("mixw_t_ready"), 1)

            with pe.Fori(0, EXPERTS // 2) as pair:
                for odd in range(2):
                    start = pe.value_load(meta[0:1, bass.ds(2 * pair + odd, 1)], min_val=0, max_val=ASSIGNED)
                    passes = pe.value_load(meta[0:1, bass.ds(EXPERTS + 2 * pair + odd, 1)], min_val=1, max_val=T // WIN)
                    before = pe.value_load(meta[0:1, bass.ds(2 * EXPERTS + 2 * pair + odd, 1)], min_val=0,
                                           max_val=EXPERTS + ASSIGNED // WIN)
                    n0 = FIRST_SLOTS + EXPERT_SLOTS * odd

                    def weight(i):
                        at = i % PER_SLOT * P
                        return ring[:, (n0 + i // PER_SLOT) % RING, at:at + P]

                    for i in range(EXPERT_SLOTS):
                        arrived(n0 + i, pair)
                    settled(pe)
                    with pe.Fori(0, passes) as w:
                        at = nc.s_assert_within(start + WIN * w, 0, ASSIGNED,
                                                skip_runtime_bounds_check_because="it begins at an assigned token")
                        for m in range(8):
                            for k in range(KB):
                                last = pe.matmul(ps[m // 4][:, m % 4 * WIN:(m % 4 + 1) * WIN], weight(m * KB + k),
                                                 xs[:, k, bass.ds(at, WIN)], start=k == 0, stop=k == KB - 1)
                        last.then_inc(S("up_done"), 1)
                        pe.wait_ge(S("hid_ready"), before + w + 1)
                        for j in range(KB):
                            for k in range(4):
                                last = pe.matmul(ps[2 + j // 4][:, j % 4 * WIN:(j % 4 + 1) * WIN], weight(64 + j * 4 + k),
                                                 two["hid"][:, k, :], start=k == 0, stop=k == 3)
                        last.then_inc(S("down_done"), 1)

            pe.wait_ge(S("moe_done"), 1)
            for i in range(ASSIGNED // P):
                for k in range(KB):
                    b = 2 * (i % 2) + k // 4
                    if i >= 2 and k % 4 == 0:
                        pe.wait_ge(S("ys_tok_copied"), 2 * (i - 2) + k // 4 + 1)
                    last = pe.transpose(ps[b][:, k % 4 * P:(k % 4 + 1) * P], ys[:, k, i * P:(i + 1) * P], ident)
                    if k % 4 == 3:
                        last.then_inc(S("ys_tok_done"), 1)
            pe.wait_ge(S("ys_tok_copied"), 2 * (ASSIGNED // P))
            for k in range(KB):
                for i in range(ASSIGNED // P):
                    last = pe.matmul(half(4 + k // 2, k % 2), ys_tok[:, i, k * P:(k + 1) * P], mixw_t[:, i, :],
                                     start=i == 0, stop=i == ASSIGNED // P - 1)
            last.then_inc(S("wide_done"), 1)
            pe.wait_ge(S("x_updates"), 2)
            column_sums(0, x_t)
            pe.wait_ge(S("sq_ready"), 2)
            column_sums(1, sq)

            def norm_sum(value):
                pe.wait_ge(S("sq_ready"), 2 + value)
                column_sums(0, sq)

            def product(out_ap, a_hi, a_lo, b_hi, b_lo, start, stop, **flags):
                first = pe.matmul(out_ap, a_hi, b_hi, start=start, stop=False, **flags)
                pe.matmul(out_ap, a_hi, b_lo, start=False, stop=False, **flags)
                return first, pe.matmul(out_ap, a_lo, b_hi, start=False, stop=stop, **flags)

            def weight_product(out_ap, q, at, b_hi, b_lo, start, stop, **flags):
                return product(out_ap, w_hi[:, q % 2, at:at + P], w_lo[:, q % 2, at:at + P], b_hi, b_lo,
                               start, stop, **flags)

            with pe.Fori(0, LAYERS) as layer:
                def part_ready(q, part, g=0):
                    pe.wait_ge(S("lo_ready"), 2 * LAYER_SLOTS * layer + 2 * q + (1 if part == "A" else 2) + 16 * g)

                def streamed(out_ap, q0, i, k, last):
                    q = q0 + i // PER_SLOT
                    if i % PER_SLOT in (0, PART_A):
                        part_ready(q, "A" if i % PER_SLOT == 0 else "B")
                    m0, m = weight_product(out_ap, q, i % PER_SLOT * P, h_hi[:, k, :], h_lo[:, k, :],
                                           start=k == 0, stop=k == KB - 1)
                    if i % PER_SLOT == 0:
                        m0.then_inc(S("a_begun"), 1)
                    if last:
                        m.then_inc(S(last), 1)

                def swiglu(at, f, norm):
                    def gate_up(c, g=0):
                        part_ready(at + c, "A", g)
                        pe.wait_ge(S("hid_made"), 2 * CHUNKS * layer + f * CHUNKS + c + 1 + 8 * g)
                        for side in range(2):
                            for k in range(KB):
                                if c == 0 and side == 0:
                                    norm_block(norm, k)
                                m0, m = weight_product(half(c % 4, side), at + c, (side * KB + k) * P, h_hi[:, k, :],
                                                       h_lo[:, k, :], start=k == 0, stop=k == KB - 1)
                                if side == 0 and k == 0:
                                    m0.then_inc(S("a_begun"), 1)
                        m.then_inc(S("gate_up_done"), 1)

                    def down(c, g=0, first=False, last=False):
                        part_ready(at + c, "B", g)
                        pe.wait_ge(S("hid_made"), 2 * CHUNKS * layer + f * CHUNKS + c + 5 + 8 * g)
                        for j in range(KB):
                            _, m = weight_product(half(4 + j // 2, j % 2), at + c, (2 * KB + j) * P,
                                                  hid_hi[:, c % 2, :], hid_lo[:, c % 2, :],
                                                  start=first and j % 2 == 0, stop=last, skip_group_check=True)
                        if last:
                            m.then_inc(S("wide_done"), 1)

                    gate_up(0)
                    gate_up(1)
                    down(0, first=True)
                    with pe.Fori(0, 2) as g:
                        for i in range(RING):
                            gate_up(2 + i, g)
                            down(1 + i, g)
                    for c in range(18, CHUNKS):
                        gate_up(c)
                        down(c - 1)
                    down(CHUNKS - 1, last=True)

                def norm_block(norm, k):
                    pe.wait_ge(S("h_ready"), KB * 3 * layer + KB * (norm - 1) + k + 1)

                norm_sum(3 * layer + 1)
                swiglu(0, 0, 1)
                norm_sum(3 * layer + 2)

                for u in range(LAYER_UNITS):
                    if u >= 4:
                        pe.wait_ge(S("proj_read"), FIRST_UNITS + LAYER_UNITS * layer + u - 3)
                    if u < V_SLOTS:
                        part_ready(MIX_AT + u, "A")
                        side = (MIX_AT + u) % 2
                        for j in range(TT):
                            tokens = slice(j * P, (j + 1) * P)
                            for k in range(KB):
                                if u == 0 and j == 0:
                                    norm_block(2, k)
                                cols = slice(k * VCOLS, (k + 1) * VCOLS)
                                m0, m = product(half(u % 4, j), h_hi[:, k, tokens], h_lo[:, k, tokens],
                                                w_hi[:, side, cols], w_lo[:, side, cols], start=k == 0, stop=k == KB - 1)
                                if j == 0 and k == 0:
                                    m0.then_inc(S("a_begun"), 1)
                        m.then_inc(S("proj_done"), 1)
                        if u == 0:
                            for j in range(TT):
                                for k in range(KB):
                                    at = late_at["forget"][0] + k * 8
                                    pe.matmul(ps[4][:, j * 8:j * 8 + 8], h_t[:, k, j * P:(j + 1) * P],
                                              three["late"][:, bass.ds(at + KB * 8 * layer, 8)], start=k == 0, stop=False)
                                m = pe.matmul(ps[4][:, j * 8:j * 8 + 8], ones[0:1, :],
                                              rows[0:1, bass.ds(r_at["forget"][0] + 8 * layer, 8)],
                                              start=False, stop=True)
                            m.then_inc(S("forget_done"), 1)
                    else:
                        for side in range(2):
                            b = 2 * (u - V_SLOTS) + side
                            for k in range(KB):
                                streamed(half(u % 4, side), MIX_AT + V_SLOTS, b * KB + k, k,
                                         "proj_done" if side == 1 and k == KB - 1 else None)
                pe.wait_ge(S("lam_ready"), layer + 1)
                pe.wait_ge(S("forget_shifted"), layer + 1)
                pe.matmul(ps[4][:, 256:258], ones[0:DH, :], lams[0:DH, 0:2], start=True, stop=True)\
                    .then_inc(S("lam_done"), 1)
                pe.wait_ge(S("log_f_ready"), layer + 1)
                tri = const("tri")
                pe.matmul(ps[5][0:8, 0:P], ffs[:, 5, 0, :], tri, start=True, stop=True)
                pe.matmul(ps[5][0:8, P:T], ffs[:, 5, 0, :], ones, start=True, stop=False)
                pe.matmul(ps[5][0:8, P:T], ffs[:, 5, 1, :], tri, start=False, stop=True)\
                    .then_inc(S("cum_done"), 1)
                for r in range(4):
                    pe.wait_ge(S("proj_read"), FIRST_UNITS + LAYER_UNITS * layer + V_SLOTS + 4 + r + 1)
                    if r >= 2:
                        pe.wait_ge(S("rope_done"), 4 * layer + r - 1)
                    for side in range(2):
                        m = pe.matmul(half(6 + r % 2, side), const("rot"), qk[:, 8 + 2 * r + side, :],
                                      start=True, stop=True)
                    m.then_inc(S("rotated"), 1)
                pe.wait_ge(S("rope_done"), 4 * layer + 4)
                pe.wait_ge(S("ncum_ready"), layer + 1)
                attention("layer", 8 + 16 * layer, 8 + 12 * layer)
                pe.wait_ge(S("od_sq_ready"), layer + 1)
                for h in range(4):
                    m = pe.matmul(half(6 + h // 2, h % 2), ones, sq[:, h, :], start=True, stop=True)
                m.then_inc(S("od_sum_ready"), 1)
                pe.wait_ge(S("mix_in_ready"), layer + 1)
                for j in range(KB):
                    for k in range(KB):
                        streamed(half(4 + j // 2, j % 2), MIX_AT + V_SLOTS, (16 + j) * KB + k, k,
                                 "wide_done" if j == k == KB - 1 else None)
                norm_sum(3 * layer + 3)
                swiglu(FFN2_AT, 1, 3)
            norm_sum(3 * LAYERS + 1)

        MIX_STEPS = {u: [MIX_AT + u + 1] for u in range(V_SLOTS)}
        for s in range(1, 6):
            MIX_STEPS.setdefault(V_SLOTS + s * PER_SLOT // 16 - 1, []).append(MIX_AT + V_SLOTS + s)

        def over_chunks(eng, body):
            body(0, 0)
            body(1, 0)
            with eng.Fori(0, 2) as g:
                for i in range(RING):
                    body(2 + i, RING * g)
            for c in range(18, CHUNKS):
                body(c, 0)

        @block.scalar
        def _(act):
            own = Chain(act, S("act_own"))

            def root(name, value, out_ap, in_ap, told):
                act.wait_ge(S(name), value)
                act.activation(out_ap, in_ap, ACT.Sqrt).then_inc(S(told), 1)

            def squares(waited, value):
                act.wait_ge(S(waited), value)
                act.activation(sq[:], x_t[:], ACT.Square).then_inc(S("sq_ready"), 1)

            def attention(kind, s0, o0):
                scores, outs = attention_units(kind)
                for s in range(len(scores) + 2):
                    if s < len(scores):
                        act.wait_ge(S("negmax_ready"), s0 + s + 1)
                        for j in range(TT):
                            p = probs[:, s % 4, j, :]
                            m = act.activation(p, p, ACT.Exp, bias=small[:, s % 4, 1, j:j + 1],
                                               accum_out=small[:, s % 4, 2, j:j + 1])
                        m.then_inc(S("exp_ready"), 1)
                    for o, (end, _) in enumerate(outs):
                        if end == s - 2:
                            act.wait_ge(S("turned"), o0 + o + 1)
                            if o >= 2:
                                act.wait_ge(S("o_ready"), o0 + o - 1)
                            act.copy(probs_t[:, o % 2, :, :], halves(2 + o % 2)).then_inc(S("turned_copied"), 1)

            act.wait_ge(S("lb_shifted"), 1)
            act.activation(lbs[:, 4:12], lbs[:, 4:12], ACT.Exp).then_inc(S("lb_exp"), 1)
            act.wait_ge(S("lb_ready"), 1)
            act.wait_ge(S("params_loaded"), 16)
            for u, (what, b0) in enumerate(projection_units()):
                act.wait_ge(S("proj_done"), u + 1)
                if what == "v":
                    m = act.copy(vtok[:, :, b0 * VCOLS:(b0 + 1) * VCOLS], halves(u % 4))
                for side in range(2 if what == "t" else 0):
                    b = b0 + side
                    src, by = ps[u % 4][:, side * T:(side + 1) * T], param("b_in", b)
                    if b < 4:
                        m = act.activation(q_hg[:, b, :], src, ACT.Silu, bias=by)
                    elif b < 8:
                        act.activation(f_hg[:, b - 4, :], src, ACT.Sigmoid, bias=by)
                        m = act.activation(k_hg[:, b - 4, :], src, ACT.Sigmoid, bias=negb[:, b - 4:b - 3], scale=-1.0)
                    elif b < 12:
                        m = act.activation(g_hg[:, b - 8, :], src, ACT.Silu, bias=by)
                    elif b < 16:
                        m = act.activation(mq[:, b - 12, :], src, ACT.Identity, bias=lbs[:, 8 + b:9 + b],
                                           scale=DH ** -0.5)
                    elif b < 20:
                        m = act.activation(mk[:, b - 16, :], src, ACT.Identity, bias=by)
                    else:
                        m = act.activation(gates[:, b - 20, :], src, ACT.Sigmoid, bias=by)
                m.then_inc(S("proj_read"), 1)

            act.wait_ge(S("hg_o_ready"), 1)
            for i in range(2):
                act.activation(sq[:, 2 * i:2 * i + 2, :], halves(6 + i), ACT.Square)
                m = act.copy(grow[:, 2 * i:2 * i + 2, :], halves(6 + i))
            m.then_inc(S("hg_sq_ready"), 1)
            root("hg_var_ready", 1, sq[:, 4:8, :], sq[:, 4:8, :], "hg_std_ready")

            attention("moba", 0, 0)

            squares("centred", 1)
            root("var_ready", 1, stat[:, 2, :], stat[:, 1, :], "std_ready")
            act.wait_ge(S("group_shifted"), 1)
            shifted = routing[:, 896:896 + TT * GROUPS]
            act.activation(shifted, shifted, ACT.Exp).then_inc(S("group_exp"), 1)
            act.wait_ge(S("second_shifted"), 1)
            second = routing[:, 960:960 + TT]
            act.activation(second, second, ACT.Exp).then_inc(S("second_exp"), 1)
            act.wait_ge(S("x_tok_done"), 1)
            for j in range(TT):
                for i in range(2):
                    m = act.copy(vtok[:, j, i * 512:(i + 1) * 512], ps[4 + 2 * j + i][:, :])
            m.then_inc(S("x_tok_ready"), 1)
            for k in range(KB):
                act.wait_ge(S("gathered"), k + 1)
                act.copy(xs[:, k, 0:ASSIGNED], ps[4 + k % 4][:, :]).then_inc(S("xs_ready"), 1)
            act.wait_ge(S("meta_ready"), 1)
            with act.Fori(0, EXPERTS) as e:
                passes = act.value_load(meta[0:1, bass.ds(EXPERTS + e, 1)], min_val=1, max_val=T // WIN)
                before = act.value_load(meta[0:1, bass.ds(2 * EXPERTS + e, 1)], min_val=0,
                                        max_val=EXPERTS + ASSIGNED // WIN)
                with act.Fori(0, passes) as w:
                    act.wait_ge(S("up_done"), before + w + 1)
                    act.activation(two["sg"], ps[0][:, :], ACT.Silu).then_inc(S("moe_silu"), 1)
            for n in range(2 * (ASSIGNED // P)):
                act.wait_ge(S("ys_tok_done"), n + 1)
                i, k = n // 2, n % 2
                act.copy(ys_tok[:, i, k * 512:(k + 1) * 512], ps[2 * (i % 2) + k][:, :])\
                    .then_inc(S("ys_tok_copied"), 1)
            squares("centred", 2)
            root("var_ready", 2, stat[:, 2, :], stat[:, 1, :], "std_ready")

            def norm(value, split=True):
                squares("x_updates", 2 + value)
                root("var_ready", 2 + value, stat[:, 2, :], stat[:, 1, :], "std_ready")
                for b in range(KB if split else 0):
                    act.wait_ge(S("h_made"), KB * (value - 1) + b + 1)
                    settled(act)
                    act.copy(h_hi[:, b, :], h_t[:, b, :]).then_inc(S("h_hi_ready"), 1)

            def hi_part(layer, q, part, more=0, counts=1):
                lo, hi = (0, PART_A * P) if part == "A" else (PART_A * P, SLOT)
                if part == "A":
                    act.wait_ge(layer_full[q % 4], 16 * (LAYER_SLOTS // 4) * layer + 16 * (q // 4 + 1) + 4 * more)
                settled(act)
                act.copy(w_hi[:, q % 2, lo:hi], ring[:, RAW[q % 4], lo:hi]).then_inc(S("hi_ready"), counts)

            def split_step(layer, q, more=0):
                act.wait_ge(S("a_begun"), LAYER_SLOTS * layer + q + 1 + more)
                token_major = MIX_AT <= q < MIX_AT + V_SLOTS
                if not token_major:
                    hi_part(layer, q, "B", more)
                if q < LAYER_SLOTS - 1:
                    hi_part(layer, q + 1, "A", more, 2 if token_major else 1)

            def swiglu(layer, f):
                at = FFN2_AT * f

                def gate(c, more):
                    n = 2 * CHUNKS * layer + CHUNKS * f + c + more
                    act.wait_ge(S("gate_up_done"), n + 1)
                    act.wait_ge(S("hid_made"), n + 3)
                    act.activation(three["sg"][:, c % 2, :], ps[c % 4][:, 0:T], ACT.Silu).then_inc(S("silu_done"), 1)
                    if c < CHUNKS - 1:
                        split_step(layer, at + c + 1, more)
                split_step(layer, at)
                over_chunks(act, gate)

            own.restart()
            with act.Fori(0, LAYERS) as layer:
                hi_part(layer, 0, "A")
                norm(3 * layer + 1)
                swiglu(layer, 0)
                norm(3 * layer + 2)
                split_step(layer, MIX_AT)
                for u in range(LAYER_UNITS):
                    act.wait_ge(S("proj_done"), FIRST_UNITS + LAYER_UNITS * layer + u + 1)
                    if u < V_SLOTS:
                        m = act.copy(vtok[:, :, u * VCOLS:(u + 1) * VCOLS], halves(u % 4))
                    else:
                        b = 2 * (u - V_SLOTS)
                        m = act.activation(qk[:, b:b + 2, :], halves(u % 4), ACT.Copy,
                                           scale=DH ** -0.5 if b % 8 < 4 else 1.0)
                    m.then_inc(S("proj_read"), 1)
                    if u == 1:
                        act.wait_ge(S("forget_shifted"), layer + 1)
                        own(act.activation(ffs[:, 2, :, :], ffs[:, 1, :, :], ACT.Exp))
                        act.activation(ffs[:, 4, :, :], ffs[:, 2, :, :], ACT.Ln, bias=1.0)\
                            .then_inc(S("forget_log"), 1)
                    for q in MIX_STEPS.get(u, ()):
                        split_step(layer, q)
                act.wait_ge(S("lam_done"), layer + 1)
                act.activation(lams[:, 2:4], ps[4][:, 256:258], ACT.Exp).then_inc(S("lam_exp"), 1)
                attention("layer", 8 + 16 * layer, 8 + 12 * layer)
                act.wait_ge(S("o_copied"), 8 + 12 * layer + 12)
                act.activation(sq[:, 0:4, :], od[:], ACT.Square).then_inc(S("od_sq_ready"), 1)
                act.copy(h_hi[:, 0:4, :], h_t[:, 0:4, :]).then_inc(S("fox_hi_ready"), 1)
                root("od_var_ready", layer + 1, sq[:, 4:8, :], sq[:, 4:8, :], "od_std_ready")
                act.wait_ge(S("diff_made"), layer + 1)
                settled(act)
                act.copy(h_hi[:, 4:8, :], h_t[:, 4:8, :]).then_inc(S("diff_hi_ready"), 1)
                split_step(layer, MIX_AT + V_SLOTS + 6)
                split_step(layer, MIX_AT + V_SLOTS + 7)
                norm(3 * layer + 3)
                swiglu(layer, 1)
                own.restart()
            norm(3 * LAYERS + 1, split=False)

        @block.vector
        def _(dve):
            own = Chain(dve, S("dve_own"))
            tt, ts, stt = dve.tensor_tensor, dve.tensor_scalar, dve.scalar_tensor_tensor

            def over(a, n, where=1):
                v = a.unsqueeze(where)
                return v.to_broadcast([*v.shape[:where], n, *v.shape[where + 1:]])

            def attention(kind, s0, o0):
                scores, outs = attention_units(kind)

                def scores_in(s):
                    what, h = scores[s]
                    dve.wait_ge(S("score_done"), s0 + s + 1)
                    if s >= 4:
                        o = next(i for i, (end, _) in enumerate(outs) if end >= s - 4)
                        dve.wait_ge(S("turned"), o0 + o + 1)
                    settled(dve)
                    for j in range(TT):
                        add = bias[:, h, P * (1 - j):P * (1 - j) + T] if what == "m" else \
                            late("causal")[:, j * T:(j + 1) * T]
                        m = dve.tensor_tensor_reduce(out=probs[:, s % 4, j, :], in0=ps[s % 2][:, j * T:(j + 1) * T],
                                                     in1=add, scale=1.0, scalar=-3e38, op0=ALU.add, op1=ALU.max,
                                                     accum_out=small[:, s % 4, 0, j:j + 1])
                    m.then_inc(S("score_read"), 1)
                    dve.wait_ge(S("score_read"), s0 + s + 1)
                    ts(small[:, s % 4, 1, :], small[:, s % 4, 0, :], -1.0, None, ALU.mult)\
                        .then_inc(S("negmax_ready"), 1)

                def reciprocals(s):
                    what, c = scores[s]
                    dve.wait_ge(S("exp_ready"), s0 + s + 1)
                    r = small[:, s % 4, 3, :]
                    if what == "d" and c % 2:
                        own(dve.reciprocal(r, small[:, s % 4, 2, :]))
                        ts(r, r, lams[:, 4:5], None, ALU.mult).then_inc(S("recip_ready"), 1)
                    else:
                        dve.reciprocal(r, small[:, s % 4, 2, :]).then_inc(S("recip_ready"), 1)

                def output(o):
                    what, h = outs[o][1]
                    dve.wait_ge(S("o_ready"), o0 + o + 1)
                    if what == "d":
                        dst, po, w = od[:, h, :], 0, P
                    else:
                        po, w = DH * (h % 2), DH
                        dst = h_t[po:po + w, h // 2 + (4 if what == "m" else 0), :]
                    dve.tensor_copy(dst, ps[4 + o % 2][po:po + w, 0:T]).then_inc(S("o_copied"), 1)

                for s in range(len(scores) + 3):
                    if s < len(scores):
                        scores_in(s)
                    if 1 <= s <= len(scores):
                        reciprocals(s - 1)
                    for o, (end, _) in enumerate(outs):
                        if end == s - 3:
                            output(o)

            def residual(value, x_by, by, told=True):
                dve.wait_ge(S("wide_done"), value)
                for b in range(4):
                    xb, pb = x_t[:, 2 * b:2 * b + 2, :], halves(4 + b)
                    if by == 1.0:
                        m = stt(xb, xb, x_by, pb, ALU.mult, ALU.add)
                    else:
                        m = stt(xb, pb, by, xb, ALU.mult, ALU.add)
                m.then_inc(S("x_updates"), 1)

            def rms_stat(value, bank=0):
                dve.wait_ge(S("sum_ready"), 4 + value)
                ts(stat[:, 1, :], ps[bank][:, 0:T], 1.0 / D, EPS, ALU.mult, ALU.add).then_inc(S("var_ready"), 1)
                dve.wait_ge(S("std_ready"), 2 + value)
                own(dve.reciprocal(stat[:, 3, :], stat[:, 2, :]))

            def norm(value, gain_of, split=True):
                rms_stat(value)
                for b in range(KB + 1):
                    if b < KB:
                        stt(h_t[:, b, :], x_t[:, b, :], gain_of(b), stat[:, 3, :], ALU.mult, ALU.mult)\
                            .then_inc(S("h_made"), 1)
                    if split and b:
                        dve.wait_ge(S("h_hi_ready"), KB * (value - 1) + b)
                        settled(dve)
                        tt(h_lo[:, b - 1, :], h_t[:, b - 1, :], h_hi[:, b - 1, :].bitcast(F32), ALU.subtract)\
                            .then_inc(S("h_ready"), 1)

            def lo_part(layer, q, part, more=0, counts=1):
                lo, hi = (0, PART_A * P) if part == "A" else (PART_A * P, SLOT)
                dve.wait_ge(S("hi_ready"), 2 * LAYER_SLOTS * layer + 2 * q + (1 if part == "A" else 2) + 2 * more)
                settled(dve)
                tt(w_lo[:, q % 2, lo:hi], ring[:, RAW[q % 4], lo:hi], w_hi[:, q % 2, lo:hi].bitcast(F32),
                   ALU.subtract).then_inc(S("lo_ready"), counts)

            def split_step(layer, q, more=0):
                token_major = MIX_AT <= q < MIX_AT + V_SLOTS
                if not token_major:
                    lo_part(layer, q, "B", more)
                if q < LAYER_SLOTS - 1:
                    lo_part(layer, q + 1, "A", more, 2 if token_major else 1)

            def layer_norm(n, g, b, told):
                dve.wait_ge(S("x_updates"), n)
                dve.wait_ge(S("sum_ready"), 2 * n - 1)
                own(ts(stat[:, 0, :], ps[0][:, 0:T], 1.0 / D, None, ALU.mult))
                tt(x_t[:], x_t[:], over(stat[:, 0, :], KB), ALU.subtract).then_inc(S("centred"), 1)
                dve.wait_ge(S("sum_ready"), 2 * n)
                ts(stat[:, 1, :], ps[1][:, 0:T], 1.0 / D, EPS, ALU.mult, ALU.add).then_inc(S("var_ready"), 1)
                dve.wait_ge(S("std_ready"), n)
                own(dve.reciprocal(stat[:, 3, :], stat[:, 2, :]))
                own(tt(x_t[:], x_t[:], over(stat[:, 3, :], KB), ALU.mult))
                for k in range(KB):
                    m = ts(x_t[:, k, :], x_t[:, k, :], param(g, k), param(b, k), ALU.mult, ALU.add)
                m.then_inc(S(told), 1)

            dve.wait_ge(S("params_loaded"), 16)
            l0, l1 = param("lb", 0, 4), param("lb", 4, 4)
            own(tt(lbs[:, 0:4], l0, l1, ALU.max))
            tt(lbs[:, 4:8], l0, lbs[:, 0:4], ALU.subtract)
            tt(lbs[:, 8:12], l1, lbs[:, 0:4], ALU.subtract).then_inc(S("lb_shifted"), 1)
            ts(negb[:], param("b_in", 4, 4), -1.0, None, ALU.mult)
            dve.wait_ge(S("lb_exp"), 1)
            own(tt(lbs[:, 0:4], lbs[:, 4:8], lbs[:, 8:12], ALU.add))
            own(dve.reciprocal(lbs[:, 8:12], lbs[:, 0:4]))
            own(tt(lbs[:, 12:16], lbs[:, 4:8], lbs[:, 8:12], ALU.mult))
            own(ts(lbs[:, 16:20], lbs[:, 12:16], -1.0, 1.0, ALU.mult, ALU.add))
            ts(lbs[:, 20:24], param("b_in", 12, 4), DH ** -0.5, None, ALU.mult).then_inc(S("lb_ready"), 1)
            dve.wait_ge(S("bias_row_done"), 1)
            dve.tensor_copy(bias_row[:, 0:T], ps[5][0:8, 0:T]).then_inc(S("bias_row_ready"), 1)

            dve.wait_ge(S("proj_read"), 4)
            for h in range(HG_HEADS):
                ts(f_hg[:, h, :], f_hg[:, h, :], lbs[:, 16 + h:17 + h], lbs[:, 12 + h:13 + h], ALU.mult, ALU.add)
                m = ts(k_hg[:, h, :], k_hg[:, h, :], lbs[:, 16 + h:17 + h], None, ALU.mult)
            own(m)

            def subs(a):
                return a.rearrange("p h (n t) -> p (h n) t", t=SUB)

            q, f, k, g = subs(q_hg), subs(f_hg), subs(k_hg), subs(grow)
            dve.wait_ge(S("band_p_zero"), 1)
            for d in range(SUB):
                p = subs(band_p[:, d % 2, :, :])
                if d:
                    dve.wait_ge(S("band_p_ready"), d)
                if d == 1:
                    own(tt(g[:, :, 1:], q[:, :, 1:], f[:, :, 1:], ALU.mult))
                elif d > 1:
                    own(tt(g[:, :, d:], g[:, :, d:], f[:, :, 1:SUB + 1 - d], ALU.mult))
                    dve.wait_ge(S("band_done"), d - 1)
                now = q if d == 0 else g
                tt(p[:, :, 0:SUB - d], now[:, :, d:], k[:, :, 0:SUB - d], ALU.mult).then_inc(S("band_p_ready"), 1)
            own(dve.tensor_copy(g[:, :, 0], f[:, :, 0]))
            for t in range(1, SUB):
                own(tt(g[:, :, t], g[:, :, t - 1], f[:, :, t], ALU.mult))
            tt(q, q, g, ALU.mult)
            own(tt(k[:, :, SUB - 2], k[:, :, SUB - 2], f[:, :, SUB - 1], ALU.mult))
            own(dve.tensor_copy(decays[:, 0, :], f[:, :, SUB - 1]))
            for n, t in enumerate(range(SUB - 3, -1, -1)):
                now = decays[:, (n + 1) % 2, :]
                own(tt(now, decays[:, n % 2, :], f[:, :, t + 1], ALU.mult))
                m = tt(k[:, :, t], k[:, :, t], now, ALU.mult)
            own(m)
            dve.wait_ge(S("band_done"), SUB)
            dve.tensor_copy(band[:], ps[4][:, 0:8 * SUB].rearrange("p (n d) -> p n d", n=8))\
                .then_inc(S("band_copied"), 1)
            dve.wait_ge(S("kdec_zero"), 1)
            for i in range(1, NSUB):
                if i >= 3:
                    dve.wait_ge(S("earlier_done"), i - 2)
                new, old = kdec[:, i % 2, :, :], kdec[:, (i - 1) % 2, :, :]
                at = SUB * (i - 1)
                if i > 1:
                    for h in range(HG_HEADS):
                        ts(new[:, h, 0:at], old[:, h, 0:at], grow[:, h, at + SUB - 1:at + SUB], None, ALU.mult)
                dve.tensor_copy(new[:, :, at:at + SUB], k_hg[:, :, at:at + SUB]).then_inc(S("kdec_ready"), 1)
                dve.wait_ge(S("kdec_ready"), i)
                if i == 1:
                    dve.wait_ge(S("band_copied"), 1)
                    mask = const("band").rearrange("p (d t) -> p d t", d=SUB)
                    own(tt(wide, over(band[:], SUB, 3), over(mask, 8, 1), ALU.mult))
                    own(dve.tensor_reduce(band[:], wide.rearrange("p n d t -> p n t d"), AX.X, ALU.add))
                    intra = stat[:, :, :].rearrange("p a (b t) -> p (a b t)", t=SUB)\
                        .rearrange("p (n b t) -> p n b t", n=8, t=SUB)
                    own(tt(intra, over(band[:], P // SUB, 2), over(over(const("blk"), SUB, 2), 8, 1), ALU.mult))
                    own(dve.memset(hg_scores, 0.0))
            dve.wait_ge(S("earlier_done"), NSUB - 1)
            for h in range(HG_HEADS):
                dve.tensor_copy(hg_scores[:, h, 0, SUB:], ps[4 + h][:, SUB:T])
                m = dve.tensor_copy(hg_scores[:, h, 1, P + SUB:], ps[4 + h][:, T + P + SUB:2 * T])
            own(m)
            flat = stat[:, :, :].rearrange("p a t -> p (a t)").rearrange("p (h j t) -> p h j t", h=4, j=TT)
            for j in range(TT):
                s = hg_scores[:, :, j, j * P:(j + 1) * P]
                m = tt(s, s, flat[:, :, j, :], ALU.add)
            m.then_inc(S("hg_scores_ready"), 1)
            dve.wait_ge(S("hg_sum_ready"), 1)
            for i in range(2):
                m = ts(sq[:, 4 + 2 * i:6 + 2 * i, :], halves(6 + i), 1.0 / P, EPS, ALU.mult, ALU.add)
            m.then_inc(S("hg_var_ready"), 1)
            dve.wait_ge(S("hg_std_ready"), 1)
            own(dve.reciprocal(sq[:, 4:8, :], sq[:, 4:8, :]))
            own(tt(grow, grow, sq[:, 4:8, :], ALU.mult))
            for h in range(HG_HEADS):
                m = stt(h_t[:, h, :], grow[:, h, :], param("hg_g", h), g_hg[:, h, :], ALU.mult, ALU.mult)
            own(m)

            dve.wait_ge(S("bias_loaded"), 16)
            attention("moba", 0, 0)

            for j in range(KB):
                dve.wait_ge(S("ab_done"), j + 1)
                own(tt(sq[:, j, :], ps[j % 4][:, 0:T], gates[:, j, :], ALU.mult))
                own(tt(stat[:, j % 2, :], ps[j % 4][:, T:2 * T], gates[:, KB + j, :], ALU.mult))
                tt(sq[:, j, :], sq[:, j, :], stat[:, j % 2, :], ALU.add).then_inc(S("mixed_ready"), 1)
            residual(1, ALPHA, 1.0)
            layer_norm(1, "ln1_g", "ln1_b", "router_in")

            def table(at, n):
                return routing[:, at:at + TT * n].rearrange("p (j n) -> p j n", j=TT)

            logits, e1, e2 = table(64, ROUTED), table(192, EXPERTS), table(256, EXPERTS)
            masked, keyed, pos = table(320, EXPERTS), table(384, EXPERTS), table(448, EXPERTS)
            chosen, keyed_g, shifted = table(512, GROUPS), table(544, GROUPS), table(896, GROUPS)
            penalty = table(576, GROUPS)
            gmax, rank, gsum, pgrp = (routing[:, a:a + TT] for a in (608, 610, 612, 614))
            top1, top2, den, w1, w2 = (routing[:, a:a + TT] for a in (616, 618, 620, 622, 624))
            pos1, pos2, second = (routing[:, a:a + TT] for a in (626, 628, 960))
            assigned = table(0, EXPERTS)

            def first_of(values, best, rev, key, where):
                own(tt(key, values, over(best, values.shape[2], 2), ALU.is_equal))
                own(tt(key, key, over(rev, TT), ALU.mult))
                own(dve.tensor_reduce(rank, key, AX.X, ALU.max))
                own(tt(where, key, over(rank, values.shape[2], 2), ALU.is_equal))

            dve.wait_ge(S("logits_done"), 1)
            own(dve.tensor_copy(logits, ps[2][:, 0:TT * ROUTED].rearrange("p (j n) -> p j n", j=TT)))
            lg = logits[:, :, 0:GROUPS]
            own(dve.tensor_reduce(gmax, lg, AX.X, ALU.max))
            tt(shifted, lg, over(gmax, GROUPS, 2), ALU.subtract).then_inc(S("group_shifted"), 1)
            first_of(lg, gmax, const("rev_group"), keyed_g, chosen)
            own(ts(penalty, chosen, -1.0, -NEG, ALU.add, ALU.mult))
            le = logits[:, :, GROUPS:].rearrange("p j (g e) -> p j g e", g=GROUPS)
            me = masked.rearrange("p j (g e) -> p j g e", g=GROUPS)
            own(tt(me, le, over(chosen, PER_GROUP, 3), ALU.mult))
            own(tt(me, me, over(penalty, PER_GROUP, 3), ALU.add))
            own(dve.tensor_reduce(top1, masked, AX.X, ALU.max))
            first_of(masked, top1, const("rev_expert"), keyed, e1)
            own(stt(masked, e1, 3.0 * NEG, masked, ALU.mult, ALU.add))
            own(dve.tensor_reduce(top2, masked, AX.X, ALU.max))
            tt(second, top2, top1, ALU.subtract).then_inc(S("second_shifted"), 1)
            first_of(masked, top2, const("rev_expert"), keyed, e2)
            tt(assigned, e1, e2, ALU.add).then_inc(S("assigned_ready"), 1)
            dve.wait_ge(S("group_exp"), 1)
            own(dve.tensor_reduce(gsum, shifted, AX.X, ALU.add))
            own(dve.reciprocal(pgrp, gsum))
            dve.wait_ge(S("second_exp"), 1)
            own(ts(den, second, 1.0, None, ALU.add))
            own(dve.reciprocal(den, den))
            own(tt(w1, pgrp, den, ALU.mult))
            own(tt(w2, w1, second, ALU.mult))
            dve.wait_ge(S("counts_done"), 1)
            cnt, passes = counts_t[:, 0:P], counts_t[:, P:2 * P]
            own(dve.tensor_copy(cnt, ps[3][0:EXPERTS, P:2 * P]))
            assert T == 2 * WIN
            ts(passes, cnt, WIN + 0.5, 1.0, ALU.is_gt, ALU.add).then_inc(S("counts_ready"), 1)
            dve.wait_ge(S("starts_done"), 1)
            dve.tensor_copy(meta[:], ps[2][0:1, 128:128 + 3 * EXPERTS]).then_inc(S("meta_ready"), 1)
            own(dve.tensor_copy(routing[:, 640:672], ps[2][:, 128:160]))
            own(tt(pos, ps[3][:, 0:TT * EXPERTS].rearrange("p (j n) -> p j n", j=TT),
                   over(routing[:, 640:672], TT), ALU.add))
            for e, where in ((e1, pos1), (e2, pos2)):
                own(tt(keyed, e, pos, ALU.mult))
                own(dve.tensor_reduce(where, keyed, AX.X, ALU.add))
            dve.wait_ge(S("iota_loaded"), 16)
            for j in range(TT):
                p1, p2 = pos1[:, j:j + 1], pos2[:, j:j + 1]
                own(ts(pick[:, j, :], iota, p1, None, ALU.is_equal))
                m = stt(pick[:, j, :], iota, p2, pick[:, j, :], ALU.is_equal, ALU.add)
            m.then_inc(S("pick_ready"), 1)
            for j in range(TT):
                p1, p2 = pos1[:, j:j + 1], pos2[:, j:j + 1]
                own(ts(mixw[:, j, :], iota, p1, w1[:, j:j + 1], ALU.is_equal, ALU.mult))
                own(ts(mixw_2[:, j, :], iota, p2, w2[:, j:j + 1], ALU.is_equal, ALU.mult))
                m = tt(mixw[:, j, :], mixw[:, j, :], mixw_2[:, j, :], ALU.add)
            m.then_inc(S("mixw_ready"), 1)
            dve.wait_ge(S("mixw_turned"), 1)
            for i in range(2):
                m = dve.tensor_copy(mixw_t[:, 2 * i:2 * i + 2, :], halves(i))
            m.then_inc(S("mixw_t_ready"), 1)
            dve.wait_ge(S("mixw_ready"), 1)

            with dve.Fori(0, EXPERTS) as e:
                start = dve.value_load(meta[0:1, bass.ds(e, 1)], min_val=0, max_val=ASSIGNED)
                passes_r = dve.value_load(meta[0:1, bass.ds(EXPERTS + e, 1)], min_val=1, max_val=T // WIN)
                before = dve.value_load(meta[0:1, bass.ds(2 * EXPERTS + e, 1)], min_val=0,
                                        max_val=EXPERTS + ASSIGNED // WIN)
                with dve.Fori(0, passes_r) as w:
                    at = nc.s_assert_within(start + WIN * w, 0, ASSIGNED,
                                            skip_runtime_bounds_check_because="it begins at an assigned token")
                    dve.wait_ge(S("moe_silu"), before + w + 1)
                    tt(two["hid"], two["sg"].rearrange("p (k n) -> p k n", k=4),
                       ps[1][:, :].rearrange("p (k n) -> p k n", k=4), ALU.mult)\
                        .then_inc(S("hid_ready"), 1)
                    dve.wait_ge(S("down_done"), before + w + 1)
                    for half in range(2):
                        m = dve.tensor_copy(ys[:, 4 * half:4 * half + 4, bass.ds(at, WIN)],
                                            ps[2 + half][:, :].rearrange("p (k n) -> p k n", k=4))
                    m.then_inc(S("ys_written"), 1)
            dve.memset(lams[:, 7:8], 0.0).then_inc(S("moe_done"), 1)
            residual(2, ALPHA, 1.0)
            layer_norm(2, "ln2_g", "ln2_b", "x_updates")

            dve.sem_inc(S("hid_made"), 4)
            dve.wait_ge(S("late_loaded"), 16)

            def swiglu(layer, f):
                at = FFN2_AT * f

                def hidden(c, more):
                    n = 2 * CHUNKS * layer + CHUNKS * f + c + more
                    hid = three["hid"][:, c % 2, :]
                    dve.wait_ge(S("silu_done"), n + 1)
                    dve.wait_ge(S("hid_made"), n + 3)
                    settled(dve)
                    tt(hid, three["sg"][:, c % 2, :], ps[c % 4][:, T:2 * T], ALU.mult).then_inc(S("hid_whole"), 1)
                    dve.wait_ge(S("hid_whole"), n + 1)
                    settled(dve)
                    dve.tensor_copy(hid_hi[:, c % 2, :], hid).then_inc(S("hid_hi_made"), 1)
                    dve.wait_ge(S("hid_hi_made"), n + 1)
                    settled(dve)
                    tt(hid_lo[:, c % 2, :], hid, hid_hi[:, c % 2, :].bitcast(F32), ALU.subtract)\
                        .then_inc(S("hid_made"), 1)
                    if c < CHUNKS - 1:
                        split_step(layer, at + c + 1, more)
                split_step(layer, at)
                over_chunks(dve, hidden)

            own.restart()
            with dve.Fori(0, LAYERS) as layer:
                own.mark(dve.tensor_copy(cur[:, 0:l_n], params[:, bass.ds(p_at["layers"][0] + l_n * layer, l_n)]))
                own(dve.tensor_copy(cur[:, l_n:l_n + 2], consts[:, bass.ds(c_at["lam_init"][0] + 2 * layer, 2)]))
                at = l_at["lam"][0]
                for i in range(2):
                    m = tt(lams[0:DH, i:i + 1], cur[0:DH, at + 2 * i:at + 2 * i + 1],
                           cur[0:DH, at + 2 * i + 1:at + 2 * i + 2], ALU.mult)
                m.then_inc(S("lam_ready"), 1)
                lo_part(layer, 0, "A")
                norm(3 * layer + 1, lambda b: gain("ffn1", b))
                swiglu(layer, 0)
                residual(3 + 3 * layer, 1.0, 0.5)
                norm(3 * layer + 2, lambda b: gain("mix", b))
                split_step(layer, MIX_AT)
                dve.wait_ge(S("forget_done"), layer + 1)
                z = ffs[:, 0, :, :]
                own(dve.tensor_copy(z, ps[4][:, 0:TT * 8].rearrange("p (j n) -> p j n", j=TT)))
                stt(ffs[:, 1, :, :], z, -1.0, z, ALU.mult, ALU.min).then_inc(S("forget_shifted"), 1)
                split_step(layer, MIX_AT + 1)
                dve.wait_ge(S("forget_log"), layer + 1)
                stt(ffs[:, 5, :, :], z, 0.0, ffs[:, 4, :, :], ALU.min, ALU.subtract).then_inc(S("log_f_ready"), 1)
                for q in range(MIX_AT + 2, MIX_AT + V_SLOTS + 6):
                    split_step(layer, q)
                dve.wait_ge(S("cum_done"), layer + 1)
                ts(ncum[0:8, :], ps[5][0:8, 0:T], -1.0, None, ALU.mult).then_inc(S("ncum_ready"), 1)
                dve.wait_ge(S("lam_exp"), layer + 1)
                own(stt(lams[:, 4:5], lams[:, 3:4], cur[:, l_n:l_n + 1], lams[:, 2:3], ALU.subtract, ALU.subtract))
                for r in range(4):
                    dve.wait_ge(S("rotated"), 4 * layer + r + 1)
                    pair = qk[:, 8 + 2 * r:10 + 2 * r, :]
                    turned = rotated[:, r % 2, :, :]
                    own.mark(tt(turned, halves(6 + r % 2), over(late("sin"), 2), ALU.mult))
                    own(tt(pair, pair, over(late("cos"), 2), ALU.mult))
                    tt(pair, pair, turned, ALU.add).then_inc(S("rope_done"), 1)
                attention("layer", 8 + 16 * layer, 8 + 12 * layer)
                dve.wait_ge(S("fox_hi_ready"), layer + 1)
                settled(dve)
                own.mark(tt(h_lo[:, 0:4, :], h_t[:, 0:4, :], h_hi[:, 0:4, :].bitcast(F32), ALU.subtract))
                dve.wait_ge(S("od_sum_ready"), layer + 1)
                for i in range(2):
                    m = ts(sq[:, 4 + 2 * i:6 + 2 * i, :], halves(6 + i), 1.0 / P, EPS, ALU.mult, ALU.add)
                m.then_inc(S("od_var_ready"), 1)
                dve.wait_ge(S("od_std_ready"), layer + 1)
                own(dve.reciprocal(sq[:, 4:8, :], sq[:, 4:8, :]))
                own(tt(od, od, sq[:, 4:8, :], ALU.mult))
                ts(h_t[:, 4:8, :], od, gain("subln", 0), cur[:, l_n + 1:l_n + 2], ALU.mult, ALU.mult)\
                    .then_inc(S("diff_made"), 1)
                dve.wait_ge(S("diff_hi_ready"), layer + 1)
                settled(dve)
                tt(h_lo[:, 4:8, :], h_t[:, 4:8, :], h_hi[:, 4:8, :].bitcast(F32), ALU.subtract)\
                    .then_inc(S("mix_in_ready"), 1)
                split_step(layer, MIX_AT + V_SLOTS + 6)
                split_step(layer, MIX_AT + V_SLOTS + 7)
                residual(4 + 3 * layer, 1.0, 1.0)
                norm(3 * layer + 3, lambda b: gain("ffn2", b))
                swiglu(layer, 1)
                residual(5 + 3 * layer, 1.0, 0.5)
                own.restart()
            norm(3 * LAYERS + 1, lambda b: param("final", b), split=False)


def constant_tables():
    idx = np.arange(P)
    t = np.arange(T)
    bucket = np.arange(T, dtype=np.int64)
    half = BUCKETS // 2
    d = np.maximum(bucket, 1).astype(np.float32)
    log_part = half + (np.log(d / np.float32(half)) / np.float32(math.log(MAX_DIST / half))
                       * np.float32(BUCKETS - half)).astype(np.int32)
    bucket = np.where(bucket < half, bucket, np.minimum(log_part, BUCKETS - 1))
    by_distance = (bucket[None, ::-1] == np.arange(BUCKETS)[:, None])
    rot = np.zeros((P, P))
    for m in range(P):
        if m % DH < DH // 2:
            rot[m + DH // 2, m] = -1.0
        else:
            rot[m - DH // 2, m] = 1.0
    band = (np.arange(SUB)[None, None, :] == (idx % SUB)[:, None, None] + np.arange(SUB)[None, :, None])
    init = [0.8 - 0.6 * math.exp(-0.3 * n) for n in range(LAYERS)]
    tables = {
        "ident": np.eye(P), "ones": np.ones((P, P)), "tri": idx[:, None] <= idx[None, :],
        "tri_strict": idx[:, None] < idx[None, :], "rot": rot, "band": band.reshape(P, -1),
        "blk": (idx // SUB)[:, None] == np.arange(P // SUB)[None, :],
        "rev_group": np.tile(np.arange(GROUPS, 0, -1), (P, 1)),
        "rev_expert": np.tile(np.arange(EXPERTS, 0, -1), (P, 1)),
        "bucket": np.concatenate([by_distance, np.zeros((P - BUCKETS, T))]),
        "lam_init": np.tile(np.array([[v, 1.0 - v] for v in init]).reshape(1, -1), (P, 1)),
    }
    inv = (1.0 / (np.float32(10000.0) ** (np.arange(0, DH, 2, dtype=np.float32) / np.float32(DH)))).astype(np.float32)
    angle = np.concatenate([t.astype(np.float32)[:, None] * inv[None, :]] * 2, axis=1)
    causal = np.stack([np.where(t[None, :] <= (idx + j * P)[:, None], 0.0, NEG) for j in range(TT)], 1)
    late = {"cos": np.tile(np.cos(angle).T, (2, 1)), "sin": np.tile(np.sin(angle).T, (2, 1)),
            "causal": causal.reshape(P, -1)}
    iota = np.tile(np.arange(ASSIGNED), (P, 1))
    pack = lambda names, of: np.concatenate([np.asarray(of[n], np.float32) for n in names], axis=1)
    return pack(CONSTS, tables), pack(("cos", "sin", "causal"), late), iota.astype(np.float32)


def sub_blocks(w):
    k, n = w.shape
    return w.reshape(k // P, P, n // P, P).transpose(1, 2, 0, 3)


def flat(*parts):
    return np.concatenate([p.reshape(P, -1) for p in parts], axis=1)


def slots(a, n):
    full = np.zeros((P, n * SLOT), np.float32)
    full[:, :a.shape[1]] = a
    return full.reshape(P, n, SLOT).transpose(1, 0, 2)


def token_major(w):
    out = []
    for v in range(w.shape[1] // VCOLS):
        part = w[:, v * VCOLS:(v + 1) * VCOLS].reshape(KB, P, VCOLS).transpose(1, 0, 2)
        out.append(slots(flat(part), 1))
    return np.concatenate(out)


def columns(v):
    return v.reshape(-1, P).T


FORGET = slice(3 * MB_HEADS * DH, 3 * MB_HEADS * DH + 8)


def layouts(i):
    w, b = i["w_in"][0], i["b_in"][0]
    at = {}
    first = 0
    for name, n in (("q", 512), ("f", 512), ("v", 512), ("g", 512), ("mq", 512), ("mk", 512), ("mv", 512),
                    ("ga", 1024), ("gb", 1024)):
        at[name] = slice(first, first + n)
        first += n
    early, later = ("q", "f", "g"), ("mq", "mk", "ga", "gb")
    ab = np.concatenate([sub_blocks(i["w_proj_a"][0]), sub_blocks(i["w_proj_b"][0])], axis=2)
    router = np.concatenate([i["w_group"][0], i["w_expert"][0]], axis=1).reshape(KB, P, ROUTED).transpose(1, 0, 2)
    first_w = np.concatenate([
        slots(flat(*[sub_blocks(w[:, at[n]]) for n in early]), 4),
        token_major(np.concatenate([w[:, at["v"]], w[:, at["mv"]]], axis=1)),
        slots(flat(*[sub_blocks(w[:, at[n]]) for n in later]), 8),
        slots(flat(ab, sub_blocks(i["w_out"][0]), router), 6)])
    moe_w = np.empty((MOE_SLOTS, P, SLOT), np.float32)
    for e in range(EXPERTS):
        moe_w[4 * e:4 * e + 4] = slots(flat(sub_blocks(i["w_gate_up"][0, e]), sub_blocks(i["w_down"][0, e])), 4)
    layer_w = np.empty((LAYERS * LAYER_SLOTS, P, SLOT), np.float32)
    for n in range(LAYERS):
        at_n = n * LAYER_SLOTS
        for first, name in ((0, "ffn1"), (FFN2_AT, "ffn2")):
            gu, down = i[f"{name}_w_gate_up_2"][n], i[f"{name}_w_down_2"][n]
            gate, up = sub_blocks(gu[:, :D_FF]), sub_blocks(gu[:, D_FF:])
            for c in range(CHUNKS):
                layer_w[at_n + first + c] = flat(gate[:, c], up[:, c], down[c * P:(c + 1) * P])
        w2 = i["w_in_2"][n]
        fq, fk, fv, _, dq, dk, dv = np.split(w2, np.cumsum([512, 512, 512, 8, 512, 512]), axis=1)
        m = at_n + MIX_AT
        layer_w[m:m + V_SLOTS] = token_major(np.concatenate([fv, dv], axis=1))
        layer_w[m + V_SLOTS:m + V_SLOTS + 8] = slots(
            flat(*[sub_blocks(v) for v in (fq, fk, dq, dk, i["w_out_2"][n])]), 8)
    b_in = np.concatenate([columns(b[at[n]]) for n in early + later], axis=1)
    rel = np.zeros((P, MB_HEADS), np.float32)
    rel[:BUCKETS] = i["rel_bias"]
    per_layer = []
    for n in range(LAYERS):
        lam = np.zeros((P, 4), np.float32)
        for c, name in enumerate(("lambda_q1_2", "lambda_k1_2", "lambda_q2_2", "lambda_k2_2")):
            lam[:DH, c] = i[name][n]
        per_layer += [columns(i["ffn1_norm_2"][n]), columns(i["mix_norm_2"][n]), columns(i["ffn2_norm_2"][n]),
                      columns(i["diff_subln_2"][n]), lam]
    params = np.concatenate([
        b_in, columns(i["lb_logits"][0]), columns(i["lb_logits"][1]), columns(i["hg_norm_g"][0]),
        columns(i["ln1_g"][0]), columns(i["ln1_b"][0]), columns(i["ln2_g"][0]), columns(i["ln2_b"][0]),
        rel, columns(i["final_norm_2"]), *per_layer], axis=1)
    rows = np.concatenate([i["b_group"][0], i["b_expert"][0], i["forget_bias_2"].reshape(-1)])[None]
    b_v = np.concatenate([b[at["v"]], b[at["mv"]]])[None]
    x = i["x"][0].T.reshape(KB, P, T).transpose(1, 0, 2)
    consts, late, iota = constant_tables()
    late = np.concatenate([late] + [i["w_in_2"][n][:, FORGET].reshape(KB, P, 8).transpose(1, 0, 2).reshape(P, -1)
                                    for n in range(LAYERS)], axis=1)
    return {"x": x, "first_w": first_w, "moe_w": moe_w, "layer_w": layer_w, "consts": consts, "late": late,
            "iota": iota, "params": params, "rows": rows, "b_v": b_v}


def kernel(**inputs):
    import concourse.bacc as bacc
    from concourse.bass_utils import run_bass_kernel_spmd

    nc = bacc.Bacc("TRN2", target_bir_lowering=False, num_devices=1)
    arrays = {f"{name}_dram": np.ascontiguousarray(a)
              for name, a in layouts({k: np.asarray(v) for k, v in inputs.items()}).items()}
    args = [nc.dram_tensor(name, a.shape, F32, kind="ExternalInput").ap() for name, a in arrays.items()]
    out = nc.dram_tensor("out_dram", (P, KB, T), F32, kind="ExternalOutput").ap()
    program(nc, *args, out)
    r = run_bass_kernel_spmd(nc, [arrays], core_ids=[0])
    y = r.results[0]["out_dram"]
    return np.ascontiguousarray(y.transpose(1, 0, 2).reshape(D, T).T).reshape(1, T, D)
```

```python
import math
from contextlib import ExitStack

import numpy as np

import concourse.bass as bass
from concourse import mybir

F32 = mybir.dt.float32
F32R = mybir.dt.float32r
I32 = mybir.dt.int32
ALU = mybir.AluOpType
ACT = mybir.ActivationFunctionType
AX = mybir.AxisListType

P = 128
T = 256
TT = T // P
D = 1024
KB = D // P
HG_HEADS = 4
SUB = 16
NSUB = T // SUB
MB_HEADS = 8
DH = 64
BUCKETS = 32
MAX_DIST = 128
GROUPS = 4
PER_GROUP = 8
EXPERTS = GROUPS * PER_GROUP
ROUTED = GROUPS + EXPERTS
TOP_K = 2
LAYERS = 2
D_FF = 2816
CHUNKS = D_FF // P
EPS = 1e-5
ALPHA = 2.0 ** 0.25
NEG = -1e30

PER_SLOT = 24
SLOT = PER_SLOT * P
RING = 8
RAW = (6, 7, 0, 1)
PART_A = 16
LAG = 2
VCOLS = 256
V_SLOTS = 4
T_BLOCKS = 36
FIRST_SLOTS = 16 + 6
EXPERT_SLOTS = 4
MOE_SLOTS = EXPERTS * EXPERT_SLOTS
MIX_AT = CHUNKS
FFN2_AT = MIX_AT + V_SLOTS + 8
LAYER_SLOTS = FFN2_AT + CHUNKS
LAYER_AT = FIRST_SLOTS + MOE_SLOTS
WIN = 128
ASSIGNED = T * TOP_K
ROUTER_AT = 8 * P
FIRST_UNITS = 22
LAYER_UNITS = 12
LOCAL = T + P

CONSTS = {"ident": P, "ones": P, "tri": P, "tri_strict": P, "rot": P, "band": SUB * SUB,
          "blk": P // SUB, "rev_group": GROUPS, "rev_expert": EXPERTS, "bucket": T,
          "lam_init": 2 * LAYERS}
LATE = {"cos": T, "sin": T, "causal": TT * T, "forget": LAYERS * KB * 8}
PARAMS = {"b_in": T_BLOCKS, "lb": 8, "hg_g": 4, "ln1_g": 8, "ln1_b": 8, "ln2_g": 8, "ln2_b": 8,
          "rel": 8, "final": 8, "layers": LAYERS * 29}
LAYER_PARAMS = {"ffn1": 8, "mix": 8, "ffn2": 8, "subln": 1, "lam": 4}
ROWS = {"b_router": ROUTED, "forget": LAYERS * 8}


def offsets(widths):
    at, out = 0, {}
    for name, width in widths.items():
        out[name] = (at, width)
        at += width
    return out, at


def attention_units(kind):
    if kind == "moba":
        return [("m", h) for h in range(8)], [(h, ("m", h)) for h in range(8)]
    scores = [("d", c) for c in range(8)] + [("f", h) for h in range(8)]
    return scores, [(2 * h + 1, ("d", h)) for h in range(4)] + [(8 + h, ("f", h)) for h in range(8)]


TURN, COPY, VALUES, OUTPUT = 2, 3, 4, 5

PAIRS = KB // 2


def projection_units():
    return ([("t", b) for b in range(0, 12, 2)] + [("v", v) for v in range(V_SLOTS)]
            + [("t", b) for b in range(12, T_BLOCKS, 2)])


class Chain:

    def __init__(self, eng, sem):
        self.eng, self.sem, self.n = eng, sem, 0

    def __call__(self, instruction):
        instruction.then_inc(self.sem, 1)
        self.n += 1
        self.eng.wait_ge(self.sem, self.n)

    def mark(self, instruction):
        instruction.then_inc(self.sem, 1)
        self.n += 1

    def wait(self):
        self.eng.wait_ge(self.sem, self.n)

    def restart(self):
        if self.n:
            self.eng.wait_ge(self.sem, self.n)
            self.eng.sem_clear(self.sem)
            self.n = 0


def program(nc, x_in, first_w, moe_w, layer_w, consts_in, late_in, iota_in, params_in, rows_in, b_v_in, out):
    ctx = ExitStack()
    with ctx:
        def sb(name, shape, dt=F32):
            return ctx.enter_context(nc.sbuf_tensor(name, shape, dt))

        def overlaid(name, shape, before, parts, after):
            with nc.sbuf_tensor(name, shape, F32) as first:
                pass
            sb(f"{name}_before", [P, before])
            later = [sb(part, [P, *s], F32R) for part, s in parts.items()]
            if after:
                sb(f"{name}_after", [P, after])
            return first, *later

        sems = {}

        def S(name):
            if name not in sems:
                sems[name] = ctx.enter_context(nc.semaphore(name))
            return sems[name]

        c_at, c_n = offsets(CONSTS)
        late_at, late_n = offsets(LATE)
        p_at, p_n = offsets(PARAMS)
        l_at, l_n = offsets(LAYER_PARAMS)
        r_at, r_n = offsets(ROWS)
        consts = sb("consts", [P, c_n])
        params = sb("params", [P, p_n])
        cur = sb("cur", [P, l_n + 2])
        rows = sb("rows", [1, r_n])
        ring, w_hi, w_lo = overlaid("ring", [P, RING, SLOT], 2 * SLOT,
                                    {"w_hi": (2, SLOT), "w_lo": (2, SLOT)}, 2 * SLOT)
        x_t = sb("x_t", [P, KB, T])
        h_t = sb("h_t", [P, KB, T])
        sq = sb("sq", [P, KB, T])
        stat = sb("stat", [P, 4, T])
        vtok = sb("vtok", [P, TT, D])
        probs = sb("probs", [P, 4, TT, T])
        probs_t = sb("probs_t", [P, 2, TT, T])
        small = sb("small", [P, 4, 4, TT])
        meta = sb("meta", [1, 4 * EXPERTS], I32)
        lbs = sb("lbs", [P, 24])
        negb = sb("negb", [P, 4])
        lams = sb("lams", [P, 8])
        ffs = sb("ffs", [P, 6, TT, 8])
        band = sb("band", [P, 8, SUB])
        decays = sb("decays", [P, 2, 4 * NSUB])

        AREA = 14336
        SPLIT = 2 * (KB + 2) * T
        area, h_hi, h_lo, hid_hi, hid_lo = overlaid(
            "area", [P, AREA], AREA - SPLIT,
            {"h_hi": (KB, T), "h_lo": (KB, T), "hid_hi": (2, T), "hid_lo": (2, T)}, 0)

        def carve(sizes, limit=AREA):
            at, got = 0, {}
            for name, shape in sizes.items():
                n = math.prod(shape)
                v = area[:, at:at + n]
                if len(shape) > 1:
                    names = "abcd"[:len(shape)]
                    v = v.rearrange(f"p ({' '.join(names)}) -> p {' '.join(names)}", **dict(zip(names, shape)))
                got[name] = v
                at += n
            assert at <= limit, at
            return got

        one = carve({"q": (4, T), "f": (4, T), "g": (4, T), "k": (4, T), "mq": (4, T), "mk": (4, T),
                     "gates": (16, T), "grow": (4, T), "bias": (MB_HEADS, LOCAL)})
        q_hg, f_hg, g_hg, k_hg = one["q"], one["f"], one["g"], one["k"]
        mq, mk, gates, grow, bias = one["mq"], one["mk"], one["gates"], one["grow"], one["bias"]
        b_v = gates[0:1, 0:4, :].rearrange("p a t -> p (a t)")
        band_p = probs[:, :, :, :].rearrange("p (r c) j t -> p r (c j) t", r=2)
        kdec = sq[:, :, :].rearrange("p (r h) t -> p r h t", r=2)
        hg_scores = h_t[:, :, :].rearrange("p (h j) t -> p h j t", j=TT)
        wide = h_t[:, :, :].rearrange("p n (d t) -> p n d t", d=SUB)
        bias_row = probs_t[0:8, 0, :, :].rearrange("p a t -> p (a t)")
        two = carve({"xs": (KB, ASSIGNED + WIN), "ys": (KB, ASSIGNED + WIN), "mixw_t": (ASSIGNED // P, T),
                     "sg": (4 * WIN,), "hid": (4, WIN)})
        xs, ys, mixw_t = two["xs"], two["ys"], two["mixw_t"]
        before_ys = ys.rearrange("p k n -> p (k n)")
        pick, mixw, mixw_2 = (before_ys[:, TT * ASSIGNED * i:TT * ASSIGNED * (i + 1)]
                              .rearrange("p (j n) -> p j n", j=TT) for i in range(3))
        iota = before_ys[:, 3 * TT * ASSIGNED:3 * TT * ASSIGNED + ASSIGNED]
        ys_tok = area[:, 0:ASSIGNED // P * D].rearrange("p (i n) -> p i n", i=ASSIGNED // P)
        routing = probs[:, 0:2, :, :].rearrange("p r a t -> p (r a t)")
        counts_t = probs[0:EXPERTS, 2, :, :].rearrange("p a t -> p (a t)")
        three = carve({"qk": (16, T), "rot": (2, 2, T), "od": (4, T), "ncum": (T,), "sg": (2, T),
                       "hid": (2, T), "late": (late_n,)}, AREA - SPLIT)
        qk, od, ncum, rotated = three["qk"], three["od"], three["ncum"], three["rot"]
        scratch = nc.dram_tensor("bias_rows_dram", [8, 2 * T], F32, kind="Internal").ap()
        copies = nc.dram_tensor("bias_copies_dram", [P, MB_HEADS * 2 * T], F32, kind="Internal").ap()
        ps = [ctx.enter_context(nc.psum_tensor(f"bank{i}", [P, 512], F32)) for i in range(8)]
        ring_full = [S(f"ring_full{i}") for i in range(RING)]

        def const(name, parts=P):
            at, n = c_at[name]
            return consts[0:parts, at:at + n]

        def late(name):
            at, n = late_at[name]
            return three["late"][:, at:at + n]

        def param(name, i, n=1, parts=P):
            at = p_at[name][0] + i
            return params[0:parts, at:at + n]

        def row(name, i, n):
            at = r_at[name][0] + i
            return rows[0:1, at:at + n]

        def gain(name, b):
            at = l_at[name][0] + b
            return cur[:, at:at + 1]

        def halves(bank):
            return ps[bank][:, :].rearrange("p (a t) -> p a t", a=2)

        def settled(eng):
            eng.sem_inc(S("waits_passed"), 1)

        layer_full = [S(f"layer_full{i}") for i in range(len(RAW))]
        ones, ident = const("ones"), const("ident")
        block = ctx.enter_context(nc.Block())

        @block.sync
        def _(sp):
            def fill(n, src):
                sp.dma_start(ring[:, n % RING, :], src).then_inc(ring_full[n % RING], 16)

            def slot_of(w, at):
                return w[bass.ds(at, 1)].rearrange("a p n -> (a p) n")

            sp.dma_start(x_t[:], x_in).then_inc(S("x_loaded"), 16)
            for n in range(FIRST_SLOTS + 2 * EXPERT_SLOTS):
                if n == 1:
                    sp.dma_start(params[:], params_in).then_inc(S("params_loaded"), 16)
                    sp.dma_start(rows[:], rows_in).then_inc(S("rows_loaded"), 16)
                    sp.dma_start(b_v, b_v_in).then_inc(S("b_v_loaded"), 16)
                    sp.dma_start(consts[:], consts_in).then_inc(S("consts_loaded"), 16)
                if n >= RING and n < FIRST_SLOTS + RING - LAG:
                    sp.wait_ge(S("slot_used"), n - RING + LAG + 1)
                elif n >= RING:
                    sp.wait_ge(S("logits_done"), 1)
                fill(n, first_w[n] if n < FIRST_SLOTS else moe_w[n - FIRST_SLOTS])
            sp.wait_ge(S("meta_ready"), 1)
            with sp.Fori(0, EXPERTS // 2 - 1) as pair:
                for half in range(2):
                    before = sp.value_load(meta[0:1, bass.ds(2 * EXPERTS + 2 * pair + half + 1, 1)],
                                           min_val=1, max_val=EXPERTS + ASSIGNED // WIN)
                    for i in range(EXPERT_SLOTS):
                        if i == 0:
                            sp.wait_ge(S("down_done"), before)
                        fill(FIRST_SLOTS + EXPERT_SLOTS * half + i,
                             slot_of(moe_w, 2 * EXPERT_SLOTS * (pair + 1) + EXPERT_SLOTS * half + i))
            before = sp.value_load(meta[0:1, 3 * EXPERTS - 1:3 * EXPERTS], min_val=1,
                                   max_val=EXPERTS + ASSIGNED // WIN)
            sp.wait_ge(S("down_done"), before)
            settled(sp)
            for i, place in enumerate(RAW):
                sp.dma_start(ring[:, place, :], layer_w[i]).then_inc(layer_full[i], 16)
            with sp.Fori(0, LAYERS * LAYER_SLOTS // len(RAW) - 1) as g:
                for i, place in enumerate(RAW):
                    sp.wait_ge(S("lo_ready"), 2 * len(RAW) * g + 2 * i + 2)
                    sp.dma_start(ring[:, place, :], slot_of(layer_w, len(RAW) * (g + 1) + i))\
                        .then_inc(layer_full[i], 16)
            sp.wait_ge(S("h_made"), KB * (3 * LAYERS + 1))
            sp.dma_start(out, h_t[:]).then_inc(S("stored"), 16)
            sp.wait_ge(S("stored"), 16)

        @block.gpsimd
        def _(pool):
            own = Chain(pool, S("pool_own"))
            pool.memset(probs[:], 0.0).then_inc(S("band_p_zero"), 1)
            pool.memset(sq[:], 0.0).then_inc(S("kdec_zero"), 1)
            own(pool.memset(bias_row[:, T:2 * T], NEG))
            pool.wait_ge(S("bias_row_ready"), 1)
            pool.dma_start(scratch, bias_row).then_inc(S("bias_stored"), 16)
            pool.wait_ge(S("bias_stored"), 16)
            rows_of = MB_HEADS * 2 * T
            pool.dma_start(copies, bass.AP(tensor=scratch.tensor, offset=0, ap=[[0, P], [1, rows_of]]))\
                .then_inc(S("bias_copied"), 16)
            pool.wait_ge(S("bias_copied"), 16)
            src = bass.AP(tensor=copies.tensor, offset=P - 1, ap=[[rows_of - 1, P], [2 * T, MB_HEADS], [1, LOCAL]])
            pool.dma_start(bias, src).then_inc(S("bias_loaded"), 16)

            def attention(kind, s0, o0):
                scores, outs = attention_units(kind)
                ends = [last for last, _ in outs]
                for s, (what, c) in enumerate(scores):
                    pool.wait_ge(S("recip_ready"), s0 + s + 1)
                    settled(pool)
                    for j in range(TT):
                        p = probs[:, s % 4, j, :]
                        n = pool.tensor_scalar(p, p, small[:, s % 4, 3, j:j + 1], None, ALU.mult)
                    if what != "d":
                        n.then_inc(S("probs_ready"), 1)
                    elif c % 2 == 0:
                        own.mark(n)
                    else:
                        own(n)
                        a, b = probs[:, s % 4, :, :], probs[:, (s - 1) % 4, :, :]
                        pool.tensor_tensor(a, a, b, ALU.add).then_inc(S("probs_ready"), 1)

            attention("moba", 0, 0)
            pool.wait_ge(S("router_in"), PAIRS)
            pool.dma_start(iota, iota_in).then_inc(S("iota_loaded"), 16)
            pool.memset(xs[:, :, ASSIGNED:], 0.0).then_inc(S("xs_zero"), 1)
            pool.wait_ge(S("x_updates"), 2 * PAIRS)
            pool.dma_start(three["late"], late_in).then_inc(S("late_loaded"), 16)
            own.restart()
            with pool.Fori(0, LAYERS) as layer:
                def norm_lo(norm):
                    for b in range(KB):
                        pool.wait_ge(S("h_hi_ready"), 3 * KB * layer + KB * (norm - 1) + b + 1)
                        settled(pool)
                        pool.tensor_tensor(h_lo[:, b, :], h_t[:, b, :], h_hi[:, b, :].bitcast(F32), ALU.subtract)\
                            .then_inc(S("h_ready"), 1)

                pool.wait_ge(S("hi_ready"), 2 * LAYER_SLOTS * layer + 1)
                settled(pool)
                part = slice(0, PART_A * P)
                pool.tensor_tensor(w_lo[:, 0, part], ring[:, RAW[0], part], w_hi[:, 0, part].bitcast(F32),
                                   ALU.subtract).then_inc(S("lo_ready"), 1)
                norm_lo(1)
                norm_lo(2)
                attention("layer", 8 + 16 * layer, 8 + 12 * layer)
                norm_lo(3)
                own.restart()

        @block.tensor
        def _(pe):
            def arrived(n, more=0):
                pe.wait_ge(ring_full[n % RING], 16 * (n // RING + 1) + 16 * more)
                return n % RING

            def sub_product(out_ap, n0, i, moving, **flags):
                n = n0 + i // PER_SLOT
                if i % PER_SLOT == 0:
                    arrived(n)
                at = i % PER_SLOT * P
                m = pe.matmul(out_ap, ring[:, n % RING, at:at + P], moving, **flags)
                if i % PER_SLOT == 0:
                    m.then_inc(S("slot_used"), 1)
                return m

            def half(bank, i, parts=P):
                return ps[bank][0:parts, i * T:(i + 1) * T]

            def column_sums(bank, src, told, n):
                for b in range(KB):
                    if b % 2 == 0:
                        pe.wait_ge(S(told), PAIRS * (n - 1) + b // 2 + 1)
                        settled(pe)
                    last = pe.matmul(half(bank, 0), ones, src[:, b, :], start=b == 0, stop=b == KB - 1)
                last.then_inc(S("sum_ready"), 1)

            def attention(kind, s0, o0, extra=None):
                scores, outs = attention_units(kind)

                def score(s):
                    what, h = scores[s]
                    if s >= 2:
                        pe.wait_ge(S("score_read"), s0 + s - 1)
                    po = DH * (h % 2)
                    if what == "m":
                        q, k = mq[po:po + DH, h // 2, :], mk[po:po + DH, h // 2, :]
                    else:
                        at = h // 2 + (0 if what == "d" else 8)
                        q, k = qk[po:po + DH, at, :], qk[po:po + DH, at + 4, :]
                    for j in range(TT):
                        last = pe.matmul(half(s % 2, j), q[:, j * P:(j + 1) * P], k, start=True, stop=what != "f")
                        if what == "f":
                            last = pe.matmul(half(s % 2, j), ident[0:8, h:h + 1].to_broadcast([8, P]), ncum[0:8, :],
                                             start=False, stop=True)
                    last.then_inc(S("score_done"), 1)

                def turn(o):
                    s = outs[o][0]
                    pe.wait_ge(S("probs_ready"), o0 + o + 1)
                    if o >= 2:
                        pe.wait_ge(S("turned_copied"), o0 + o - 1)
                    for i in range(TT):
                        for j in range(TT):
                            last = pe.transpose(ps[2 + o % 2][:, i * T + j * P:i * T + (j + 1) * P],
                                                probs[:, s % 4, j, i * P:(i + 1) * P], ident)
                    last.then_inc(S("turned"), 1)

                def values(o):
                    what, h = outs[o][1]
                    pe.wait_ge(S("turned_copied"), o0 + o + 1)
                    if o >= 2:
                        pe.wait_ge(S("o_copied"), o0 + o - 1)
                    if what == "d":
                        at, w, po = 512 + h * P, P, 0
                    else:
                        at, w, po = (512 if what == "m" else 0) + h * DH, DH, DH * (h % 2)
                    for i in range(TT):
                        last = pe.matmul(ps[4 + o % 2][po:po + w, 0:T], vtok[:, i, at:at + w],
                                         probs_t[:, o % 2, i, :], start=i == 0, stop=i == TT - 1)
                    last.then_inc(S("o_ready"), 1)

                for s in range(len(scores) + VALUES):
                    if s < len(scores):
                        score(s)
                    for o, (end, _) in enumerate(outs):
                        if end == s - TURN:
                            turn(o)
                        if end == s - VALUES:
                            values(o)
                    if extra and s in extra:
                        extra[s]()

            def out_product(n0, first, src):
                for j in range(KB):
                    for k in range(KB):
                        last = sub_product(half(4 + j // 2, j % 2), n0, first + j * KB + k, src[:, k, :],
                                           start=k == 0, stop=k == KB - 1)
                    if j % 2:
                        last.then_inc(S("wide_done"), 1)

            pe.wait_ge(S("x_loaded"), 16)

            def diagonal(d):
                pe.wait_ge(S("band_p_ready"), d + 1)
                for h in range(HG_HEADS):
                    for j in range(TT):
                        c = (h * TT + j) * SUB + d
                        last = pe.matmul(ps[4][:, c:c + 1], band_p[:, d % 2, h, j * P:(j + 1) * P], ones[:, 0:1],
                                         start=True, stop=True)
                last.then_inc(S("band_done"), 1)

            def earlier(i):
                if i == 1:
                    pe.wait_ge(S("band_copied"), 1)
                    pe.wait_ge(S("bias_row_ready"), 1)
                pe.wait_ge(S("kdec_ready"), i)
                for h in range(HG_HEADS):
                    for j in range(TT if i > NSUB // TT else 1):
                        last = pe.matmul(ps[4 + h][:, j * T + i * SUB:j * T + (i + 1) * SUB],
                                         kdec[:, i % 2, h, j * P:(j + 1) * P], q_hg[:, h, i * SUB:(i + 1) * SUB],
                                         start=True, stop=True)
                last.then_inc(S("earlier_done"), 1)

            between = [lambda d=d: diagonal(d) for d in range(SUB)] + [lambda i=i: earlier(i) for i in range(1, NSUB)]
            for u, (what, b) in enumerate(projection_units()):
                if u == 4:
                    for name in ("consts_loaded", "params_loaded", "rows_loaded", "b_v_loaded"):
                        pe.wait_ge(S(name), 16)
                    pe.matmul(half(5, 0, 8), param("rel", 0, 8, BUCKETS), const("bucket", BUCKETS),
                              start=True, stop=True).then_inc(S("bias_row_done"), 1)
                if u >= 4:
                    pe.wait_ge(S("proj_read"), u - 3)
                if what == "t":
                    for side in range(2):
                        first = (b + side) * KB + (V_SLOTS * PER_SLOT if b >= 12 else 0)
                        for k in range(KB):
                            last = sub_product(half(u % 4, side), 0, first + k, x_t[:, k, :],
                                               start=k == 0, stop=k == KB - 1)
                else:
                    slot = arrived(4 + b)
                    for j in range(TT):
                        for k in range(KB):
                            m = pe.matmul(half(u % 4, j), x_t[:, k, j * P:(j + 1) * P],
                                          ring[:, slot, k * VCOLS:(k + 1) * VCOLS], start=k == 0, stop=False)
                            if j == 0 and k == 0:
                                m.then_inc(S("slot_used"), 1)
                        last = pe.matmul(half(u % 4, j), ones[0:1, :], b_v[:, b * VCOLS:(b + 1) * VCOLS],
                                         start=False, stop=True)
                last.then_inc(S("proj_done"), 1)
                if u >= 6:
                    for _ in range(2):
                        if between:
                            between.pop(0)()
            for step in between:
                step()

            pe.wait_ge(S("hg_scores_ready"), 1)
            for h in range(HG_HEADS):
                for j in range(TT):
                    last = pe.matmul(half(6 + h // 2, h % 2), vtok[:, j, h * P:(h + 1) * P], hg_scores[:, h, j, :],
                                     start=j == 0, stop=j == TT - 1)
            last.then_inc(S("hg_o_ready"), 1)

            def hg_sums():
                pe.wait_ge(S("hg_sq_ready"), 1)
                for h in range(HG_HEADS):
                    last = pe.matmul(half(6 + h // 2, h % 2), ones, sq[:, h, :], start=True, stop=True)
                last.then_inc(S("hg_sum_ready"), 1)

            pe.wait_ge(S("proj_read"), FIRST_UNITS)
            attention("moba", 0, 0, {1: hg_sums})

            pe.wait_ge(S("o_copied"), MB_HEADS)
            for j in range(KB):
                if j >= 4:
                    pe.wait_ge(S("mixed_ready"), j - 3)
                for side in range(2):
                    for k in range(4):
                        last = sub_product(half(j % 4, side), 16, j * KB + side * 4 + k, h_t[:, side * 4 + k, :],
                                           start=k == 0, stop=k == 3)
                last.then_inc(S("ab_done"), 1)
            pe.wait_ge(S("mixed_ready"), KB)
            out_product(16, KB * KB, sq)
            column_sums(0, x_t, "x_updates", 1)
            column_sums(1, sq, "sq_ready", 1)

            for j in range(TT):
                out_ap = ps[2][:, j * ROUTED:(j + 1) * ROUTED]
                for k in range(KB):
                    if j == 0 and k % 2 == 0:
                        pe.wait_ge(S("router_in"), k // 2 + 1)
                    at = ROUTER_AT + k * ROUTED
                    pe.matmul(out_ap, x_t[:, k, j * P:(j + 1) * P], ring[:, (FIRST_SLOTS - 1) % RING, at:at + ROUTED],
                              start=k == 0, stop=False)
                last = pe.matmul(out_ap, ones[0:1, :], row("b_router", 0, ROUTED), start=False, stop=True)
            last.then_inc(S("logits_done"), 1)
            for j in range(TT):
                for k in range(KB):
                    last = pe.transpose(ps[4 + 2 * j + k // 4][:, k % 4 * P:(k % 4 + 1) * P],
                                        x_t[:, k, j * P:(j + 1) * P], ident)
            last.then_inc(S("x_tok_done"), 1)
            pe.wait_ge(S("assigned_ready"), 1)
            assigned = routing[:, 0:TT * EXPERTS].rearrange("p (j e) -> p j e", j=TT)
            strict = const("tri_strict")
            pe.matmul(ps[3][:, 0:EXPERTS], strict, assigned[:, 0, :], start=True, stop=True)
            pe.matmul(ps[3][:, EXPERTS:2 * EXPERTS], ones, assigned[:, 0, :], start=True, stop=False)
            pe.matmul(ps[3][:, EXPERTS:2 * EXPERTS], strict, assigned[:, 1, :], start=False, stop=True)
            pe.matmul(ps[3][0:EXPERTS, P:2 * P], assigned[:, 0, :], ones, start=True, stop=False)
            pe.matmul(ps[3][0:EXPERTS, P:2 * P], assigned[:, 1, :], ones, start=False, stop=True)\
                .then_inc(S("counts_done"), 1)
            pe.wait_ge(S("counts_ready"), 1)
            few = strict[0:EXPERTS, 0:EXPERTS]
            pe.matmul(ps[2][:, 128:128 + EXPERTS], counts_t[:, 0:P], few, start=True, stop=True)
            pe.matmul(ps[2][:, 160:160 + EXPERTS], counts_t[:, P:2 * P], ident[0:EXPERTS, 0:EXPERTS],
                      start=True, stop=True)
            pe.matmul(ps[2][:, 192:192 + EXPERTS], counts_t[:, P:2 * P], few, start=True, stop=True)\
                .then_inc(S("starts_done"), 1)
            pe.wait_ge(S("x_tok_ready"), 1)
            pe.wait_ge(S("pick_ready"), 1)
            for k in range(KB):
                if k >= 4:
                    pe.wait_ge(S("xs_ready"), k - 3)
                for j in range(TT):
                    last = pe.matmul(ps[4 + k % 4][:, :], vtok[:, j, k * P:(k + 1) * P], pick[:, j, :],
                                     start=j == 0, stop=j == TT - 1)
                last.then_inc(S("gathered"), 1)
            pe.wait_ge(S("mixw_ready"), 1)
            for i in range(ASSIGNED // P):
                for j in range(TT):
                    last = pe.transpose(ps[i // 2][:, i % 2 * T + j * P:i % 2 * T + (j + 1) * P],
                                        mixw[:, j, i * P:(i + 1) * P], ident)
            last.then_inc(S("mixw_turned"), 1)
            pe.wait_ge(S("xs_ready"), KB)
            pe.wait_ge(S("xs_zero"), 1)
            pe.wait_ge(S("mixw_t_ready"), 1)

            with pe.Fori(0, EXPERTS // 2) as pair:
                for odd in range(2):
                    packed = pe.value_load(meta[0:1, bass.ds(3 * EXPERTS + 2 * pair + odd, 1)], min_val=1,
                                           max_val=4 * 64 * ASSIGNED + 4 * 63 + T // WIN)
                    assert EXPERTS + ASSIGNED // WIN < 64 and T // WIN < 4
                    start, before, passes = packed // 256, packed // 4 % 64, packed % 4
                    n0 = FIRST_SLOTS + EXPERT_SLOTS * odd

                    def weight(i):
                        at = i % PER_SLOT * P
                        if i % PER_SLOT == 0:
                            arrived(n0 + i // PER_SLOT, pair)
                            settled(pe)
                        return ring[:, (n0 + i // PER_SLOT) % RING, at:at + P]

                    with pe.Fori(0, passes) as w:
                        at = nc.s_assert_within(start + WIN * w, 0, ASSIGNED,
                                                skip_runtime_bounds_check_because="it begins at an assigned token")
                        for m in range(8):
                            for k in range(KB):
                                last = pe.matmul(ps[m // 4][:, m % 4 * WIN:(m % 4 + 1) * WIN], weight(m * KB + k),
                                                 xs[:, k, bass.ds(at, WIN)], start=k == 0, stop=k == KB - 1)
                            if m % 4 == 3:
                                last.then_inc(S("up_done"), 1)
                        for side in range(2):
                            pe.wait_ge(S("hid_ready"), 2 * before + 2 * w + side + 1)
                            settled(pe)
                            for j in range(KB):
                                for k in range(2):
                                    last = pe.matmul(ps[2 + j // 4][:, j % 4 * WIN:(j % 4 + 1) * WIN],
                                                     weight(64 + side * 16 + j * 2 + k), two["hid"][:, 2 * side + k, :],
                                                     start=side == k == j % 4 == 0, stop=side == k == 1,
                                                     skip_group_check=True)
                        last.then_inc(S("down_done"), 1)

            pe.wait_ge(S("moe_done"), 1)
            for i in range(ASSIGNED // P):
                for k in range(KB):
                    b = 2 * (i % 2) + k // 4
                    if i >= 2 and k % 4 == 0:
                        pe.wait_ge(S("ys_tok_copied"), 2 * (i - 2) + k // 4 + 1)
                    last = pe.transpose(ps[b][:, k % 4 * P:(k % 4 + 1) * P], ys[:, k, i * P:(i + 1) * P], ident)
                    if k % 4 == 3:
                        last.then_inc(S("ys_tok_done"), 1)
            pe.wait_ge(S("ys_tok_copied"), 2 * (ASSIGNED // P))
            for k in range(KB):
                for i in range(ASSIGNED // P):
                    last = pe.matmul(half(4 + k // 2, k % 2), ys_tok[:, i, k * P:(k + 1) * P], mixw_t[:, i, :],
                                     start=i == 0, stop=i == ASSIGNED // P - 1)
                if k % 2:
                    last.then_inc(S("wide_done"), 1)
            column_sums(0, x_t, "x_updates", 2)
            column_sums(1, sq, "sq_ready", 2)

            def norm_sum(value):
                column_sums(0, sq, "sq_ready", 2 + value)

            def product(out_ap, a_hi, a_lo, b_hi, b_lo, start, stop, **flags):
                first = pe.matmul(out_ap, a_hi, b_hi, start=start, stop=False, **flags)
                pe.matmul(out_ap, a_hi, b_lo, start=False, stop=False, **flags)
                return first, pe.matmul(out_ap, a_lo, b_hi, start=False, stop=stop, **flags)

            def weight_product(out_ap, q, at, b_hi, b_lo, start, stop, **flags):
                return product(out_ap, w_hi[:, q % 2, at:at + P], w_lo[:, q % 2, at:at + P], b_hi, b_lo,
                               start, stop, **flags)

            with pe.Fori(0, LAYERS) as layer:
                def part_ready(q, part, g=0):
                    pe.wait_ge(S("lo_ready"), 2 * LAYER_SLOTS * layer + 2 * q + (1 if part == "A" else 2) + 16 * g)

                def streamed(out_ap, q0, i, k, last):
                    q = q0 + i // PER_SLOT
                    if i % PER_SLOT in (0, PART_A):
                        part_ready(q, "A" if i % PER_SLOT == 0 else "B")
                    m0, m = weight_product(out_ap, q, i % PER_SLOT * P, h_hi[:, k, :], h_lo[:, k, :],
                                           start=k == 0, stop=k == KB - 1)
                    if i % PER_SLOT == 0:
                        m0.then_inc(S("a_begun"), 1)
                    if last:
                        m.then_inc(S(last), 1)

                def swiglu(at, f, norm):
                    def gate_up(c, g=0):
                        part_ready(at + c, "A", g)
                        pe.wait_ge(S("hid_made"), 2 * CHUNKS * layer + f * CHUNKS + c + 1 + 8 * g)
                        order = [(side, k) for side in range(2) for k in range(KB)]
                        for side, k in sorted(order, key=lambda n: n[1]) if c == 0 else order:
                            if c == 0 and side == 0:
                                norm_block(norm, k)
                            m0, m = weight_product(half(c % 4, side), at + c, (side * KB + k) * P, h_hi[:, k, :],
                                                   h_lo[:, k, :], start=side == k == 0, stop=k == KB - 1,
                                                   skip_group_check=True)
                            if side == 0 and k == 0:
                                m0.then_inc(S("a_begun"), 1)
                        m.then_inc(S("gate_up_done"), 1)

                    def down(c, g=0, first=False, last=False):
                        part_ready(at + c, "B", g)
                        pe.wait_ge(S("hid_made"), 2 * CHUNKS * layer + f * CHUNKS + c + 5 + 8 * g)
                        for j in range(KB):
                            _, m = weight_product(half(4 + j // 2, j % 2), at + c, (2 * KB + j) * P,
                                                  hid_hi[:, c % 2, :], hid_lo[:, c % 2, :],
                                                  start=first and j % 2 == 0, stop=last, skip_group_check=True)
                            if last and j % 2:
                                m.then_inc(S("wide_done"), 1)

                    gate_up(0)
                    gate_up(1)
                    down(0, first=True)
                    with pe.Fori(0, 2) as g:
                        for i in range(RING):
                            gate_up(2 + i, g)
                            down(1 + i, g)
                    for c in range(18, CHUNKS):
                        gate_up(c)
                        down(c - 1)
                    down(CHUNKS - 1, last=True)

                def norm_block(norm, k):
                    pe.wait_ge(S("h_ready"), KB * 3 * layer + KB * (norm - 1) + k + 1)

                norm_sum(3 * layer + 1)
                swiglu(0, 0, 1)
                norm_sum(3 * layer + 2)

                for u in range(LAYER_UNITS):
                    if u >= 4:
                        pe.wait_ge(S("proj_read"), FIRST_UNITS + LAYER_UNITS * layer + u - 3)
                    if u < V_SLOTS:
                        part_ready(MIX_AT + u, "A")
                        side = (MIX_AT + u) % 2
                        for j in range(TT):
                            tokens = slice(j * P, (j + 1) * P)
                            for k in range(KB):
                                if u == 0 and j == 0:
                                    norm_block(2, k)
                                cols = slice(k * VCOLS, (k + 1) * VCOLS)
                                m0, m = product(half(u % 4, j), h_hi[:, k, tokens], h_lo[:, k, tokens],
                                                w_hi[:, side, cols], w_lo[:, side, cols], start=k == 0, stop=k == KB - 1)
                                if j == 0 and k == 0:
                                    m0.then_inc(S("a_begun"), 1)
                        m.then_inc(S("proj_done"), 1)
                        if u == 0:
                            for j in range(TT):
                                for k in range(KB):
                                    at = late_at["forget"][0] + k * 8
                                    pe.matmul(ps[4][:, j * 8:j * 8 + 8], h_t[:, k, j * P:(j + 1) * P],
                                              three["late"][:, bass.ds(at + KB * 8 * layer, 8)], start=k == 0, stop=False)
                                m = pe.matmul(ps[4][:, j * 8:j * 8 + 8], ones[0:1, :],
                                              rows[0:1, bass.ds(r_at["forget"][0] + 8 * layer, 8)],
                                              start=False, stop=True)
                            m.then_inc(S("forget_done"), 1)
                    else:
                        for side in range(2):
                            b = 2 * (u - V_SLOTS) + side
                            for k in range(KB):
                                streamed(half(u % 4, side), MIX_AT + V_SLOTS, b * KB + k, k,
                                         "proj_done" if side == 1 and k == KB - 1 else None)
                        if 6 <= u < 10:
                            r = u - 6
                            pe.wait_ge(S("proj_read"), FIRST_UNITS + LAYER_UNITS * layer + V_SLOTS + r + 1)
                            if r >= 2:
                                pe.wait_ge(S("rope_done"), 4 * layer + r - 1)
                            for side in range(2):
                                m = pe.matmul(half(6 + r % 2, side), const("rot"), qk[:, 2 * r + side, :],
                                              start=True, stop=True)
                            m.then_inc(S("rotated"), 1)
                pe.wait_ge(S("lam_ready"), layer + 1)
                pe.wait_ge(S("forget_shifted"), layer + 1)
                pe.matmul(ps[4][:, 256:258], ones[0:DH, :], lams[0:DH, 0:2], start=True, stop=True)\
                    .then_inc(S("lam_done"), 1)
                pe.wait_ge(S("log_f_ready"), layer + 1)
                tri = const("tri")
                pe.matmul(ps[5][0:8, 0:P], ffs[:, 5, 0, :], tri, start=True, stop=True)
                pe.matmul(ps[5][0:8, P:T], ffs[:, 5, 0, :], ones, start=True, stop=False)
                pe.matmul(ps[5][0:8, P:T], ffs[:, 5, 1, :], tri, start=False, stop=True)\
                    .then_inc(S("cum_done"), 1)
                pe.wait_ge(S("rope_done"), 4 * layer + 4)
                pe.wait_ge(S("ncum_ready"), layer + 1)

                def diff_sums(i):
                    pe.wait_ge(S("od_sq_ready"), 2 * layer + i + 1)
                    for h in (2 * i, 2 * i + 1):
                        m = pe.matmul(half(6 + i, h % 2), ones, sq[:, h, :], start=True, stop=True)
                    m.then_inc(S("od_sum_ready"), 1)

                attention("layer", 8 + 16 * layer, 8 + 12 * layer, {10: lambda: diff_sums(0), 14: lambda: diff_sums(1)})
                pe.wait_ge(S("mix_in_ready"), 4 * layer + 4)
                for j in range(KB):
                    for k in range(KB):
                        streamed(half(4 + j // 2, j % 2), MIX_AT + V_SLOTS, (16 + j) * KB + k, k,
                                 "wide_done" if j % 2 and k == KB - 1 else None)
                norm_sum(3 * layer + 3)
                swiglu(FFN2_AT, 1, 3)
            norm_sum(3 * LAYERS + 1)

        MIX_STEPS = {u: [MIX_AT + u + 1] for u in range(V_SLOTS)}
        for s in range(1, 6):
            MIX_STEPS.setdefault(V_SLOTS + s * PER_SLOT // 16 - 1, []).append(MIX_AT + V_SLOTS + s)

        def over_chunks(eng, body):
            body(0, 0)
            body(1, 0)
            with eng.Fori(0, 2) as g:
                for i in range(RING):
                    body(2 + i, RING * g)
            for c in range(18, CHUNKS):
                body(c, 0)

        @block.scalar
        def _(act):
            own = Chain(act, S("act_own"))

            def root(name, value, out_ap, in_ap, told):
                act.wait_ge(S(name), value)
                act.activation(out_ap, in_ap, ACT.Sqrt).then_inc(S(told), 1)

            def squares(waited, value):
                for p in range(PAIRS):
                    act.wait_ge(S(waited), PAIRS * (value - 1) + p + 1)
                    settled(act)
                    pair = slice(2 * p, 2 * p + 2)
                    act.activation(sq[:, pair, :], x_t[:, pair, :], ACT.Square).then_inc(S("sq_ready"), 1)

            def layer_norm(n, b, told):
                squares("centred", n)
                root("var_ready", n, stat[:, 2, :], stat[:, 1, :], "std_ready")
                for k in range(KB):
                    act.wait_ge(S("scaled"), KB * (n - 1) + k + 1)
                    m = act.activation(x_t[:, k, :], x_t[:, k, :], ACT.Identity, bias=param(b, k))
                    if k % 2:
                        m.then_inc(S(told), 1)

            def attention(kind, s0, o0, extra=None):
                scores, outs = attention_units(kind)
                for s in range(len(scores) + COPY):
                    if s < len(scores):
                        act.wait_ge(S("negmax_ready"), s0 + s + 1)
                        for j in range(TT):
                            p = probs[:, s % 4, j, :]
                            m = act.activation(p, p, ACT.Exp, bias=small[:, s % 4, 1, j:j + 1],
                                               accum_out=small[:, s % 4, 2, j:j + 1])
                        m.then_inc(S("exp_ready"), 1)
                    for o, (end, _) in enumerate(outs):
                        if end == s - COPY:
                            act.wait_ge(S("turned"), o0 + o + 1)
                            if o >= 2:
                                act.wait_ge(S("o_ready"), o0 + o - 1)
                            act.copy(probs_t[:, o % 2, :, :], halves(2 + o % 2)).then_inc(S("turned_copied"), 1)
                    if extra and s in extra:
                        extra[s]()

            act.wait_ge(S("lb_shifted"), 1)
            act.activation(lbs[:, 4:12], lbs[:, 4:12], ACT.Exp).then_inc(S("lb_exp"), 1)
            act.wait_ge(S("lb_ready"), 1)
            act.wait_ge(S("params_loaded"), 16)
            for u, (what, b0) in enumerate(projection_units()):
                act.wait_ge(S("proj_done"), u + 1)
                if what == "v":
                    m = act.copy(vtok[:, :, b0 * VCOLS:(b0 + 1) * VCOLS], halves(u % 4))
                for side in range(2 if what == "t" else 0):
                    b = b0 + side
                    src, by = ps[u % 4][:, side * T:(side + 1) * T], param("b_in", b)
                    if b < 4:
                        m = act.activation(q_hg[:, b, :], src, ACT.Silu, bias=by)
                    elif b < 8:
                        act.activation(f_hg[:, b - 4, :], src, ACT.Sigmoid, bias=by)
                        m = act.activation(k_hg[:, b - 4, :], src, ACT.Sigmoid, bias=negb[:, b - 4:b - 3], scale=-1.0)
                    elif b < 12:
                        m = act.activation(g_hg[:, b - 8, :], src, ACT.Silu, bias=by)
                    elif b < 16:
                        m = act.activation(mq[:, b - 12, :], src, ACT.Identity, bias=lbs[:, 8 + b:9 + b],
                                           scale=DH ** -0.5)
                    elif b < 20:
                        m = act.activation(mk[:, b - 16, :], src, ACT.Identity, bias=by)
                    else:
                        m = act.activation(gates[:, b - 20, :], src, ACT.Sigmoid, bias=by)
                m.then_inc(S("proj_read"), 1)

            act.wait_ge(S("hg_o_ready"), 1)
            for i in range(2):
                act.activation(sq[:, 2 * i:2 * i + 2, :], halves(6 + i), ACT.Square)
                m = act.copy(grow[:, 2 * i:2 * i + 2, :], halves(6 + i))
            m.then_inc(S("hg_sq_ready"), 1)

            attention("moba", 0, 0,
                      {3: lambda: root("hg_var_ready", 1, sq[:, 4:8, :], sq[:, 4:8, :], "hg_std_ready")})

            layer_norm(1, "ln1_b", "router_in")
            act.wait_ge(S("group_shifted"), 1)
            shifted = routing[:, 896:896 + TT * GROUPS]
            act.activation(shifted, shifted, ACT.Exp).then_inc(S("group_exp"), 1)
            act.wait_ge(S("second_shifted"), 1)
            second = routing[:, 960:960 + TT]
            act.activation(second, second, ACT.Exp).then_inc(S("second_exp"), 1)
            act.wait_ge(S("x_tok_done"), 1)
            for j in range(TT):
                for i in range(2):
                    m = act.copy(vtok[:, j, i * 512:(i + 1) * 512], ps[4 + 2 * j + i][:, :])
            m.then_inc(S("x_tok_ready"), 1)
            for k in range(KB):
                act.wait_ge(S("gathered"), k + 1)
                act.copy(xs[:, k, 0:ASSIGNED], ps[4 + k % 4][:, :]).then_inc(S("xs_ready"), 1)
            act.wait_ge(S("meta_ready"), 1)
            with act.Fori(0, EXPERTS) as e:
                passes = act.value_load(meta[0:1, bass.ds(EXPERTS + e, 1)], min_val=1, max_val=T // WIN)
                before = act.value_load(meta[0:1, bass.ds(2 * EXPERTS + e, 1)], min_val=0,
                                        max_val=EXPERTS + ASSIGNED // WIN)
                with act.Fori(0, passes) as w:
                    for side in range(2):
                        act.wait_ge(S("up_done"), 2 * before + 2 * w + side + 1)
                        act.activation(two["sg"][:, side * T:(side + 1) * T], ps[side][:, 0:T], ACT.Silu)\
                            .then_inc(S("moe_silu"), 1)
            for n in range(2 * (ASSIGNED // P)):
                act.wait_ge(S("ys_tok_done"), n + 1)
                i, k = n // 2, n % 2
                act.copy(ys_tok[:, i, k * 512:(k + 1) * 512], ps[2 * (i % 2) + k][:, :])\
                    .then_inc(S("ys_tok_copied"), 1)
            layer_norm(2, "ln2_b", "x_updates")

            def norm(value, split=True, first_slot_of=None):
                squares("x_updates", 2 + value)
                if first_slot_of is not None:
                    hi_part(first_slot_of, 0, "A")
                root("var_ready", 2 + value, stat[:, 2, :], stat[:, 1, :], "std_ready")
                for b in range(KB if split else 0):
                    act.wait_ge(S("h_made"), KB * (value - 1) + b + 1)
                    settled(act)
                    act.copy(h_hi[:, b, :], h_t[:, b, :]).then_inc(S("h_hi_ready"), 1)

            def hi_part(layer, q, part, more=0, counts=1):
                lo, hi = (0, PART_A * P) if part == "A" else (PART_A * P, SLOT)
                if part == "A":
                    act.wait_ge(layer_full[q % 4], 16 * (LAYER_SLOTS // 4) * layer + 16 * (q // 4 + 1) + 4 * more)
                settled(act)
                act.copy(w_hi[:, q % 2, lo:hi], ring[:, RAW[q % 4], lo:hi]).then_inc(S("hi_ready"), counts)

            def split_step(layer, q, more=0):
                act.wait_ge(S("a_begun"), LAYER_SLOTS * layer + q + 1 + more)
                token_major = MIX_AT <= q < MIX_AT + V_SLOTS
                if not token_major:
                    hi_part(layer, q, "B", more)
                if q < LAYER_SLOTS - 1:
                    hi_part(layer, q + 1, "A", more, 2 if token_major else 1)

            def swiglu(layer, f):
                at = FFN2_AT * f

                def gate(c, more):
                    n = 2 * CHUNKS * layer + CHUNKS * f + c + more
                    act.wait_ge(S("gate_up_done"), n + 1)
                    act.wait_ge(S("hid_made"), n + 3)
                    act.activation(three["sg"][:, c % 2, :], ps[c % 4][:, 0:T], ACT.Silu).then_inc(S("silu_done"), 1)
                    if c < CHUNKS - 1:
                        split_step(layer, at + c + 1, more)
                split_step(layer, at)
                over_chunks(act, gate)

            own.restart()
            with act.Fori(0, LAYERS) as layer:
                norm(3 * layer + 1, first_slot_of=layer)
                swiglu(layer, 0)
                norm(3 * layer + 2)
                split_step(layer, MIX_AT)
                for u in range(LAYER_UNITS):
                    act.wait_ge(S("proj_done"), FIRST_UNITS + LAYER_UNITS * layer + u + 1)
                    if u < V_SLOTS:
                        m = act.copy(vtok[:, :, u * VCOLS:(u + 1) * VCOLS], halves(u % 4))
                    else:
                        b = 2 * (u - V_SLOTS)
                        m = act.activation(qk[:, b:b + 2, :], halves(u % 4), ACT.Copy,
                                           scale=DH ** -0.5 if b % 8 < 4 else 1.0)
                    m.then_inc(S("proj_read"), 1)
                    if u == 1:
                        act.wait_ge(S("forget_shifted"), layer + 1)
                        own(act.activation(ffs[:, 2, :, :], ffs[:, 1, :, :], ACT.Exp))
                        act.activation(ffs[:, 4, :, :], ffs[:, 2, :, :], ACT.Ln, bias=1.0)\
                            .then_inc(S("forget_log"), 1)
                    for q in MIX_STEPS.get(u, ()):
                        split_step(layer, q)
                act.wait_ge(S("lam_done"), layer + 1)
                act.activation(lams[:, 2:4], ps[4][:, 256:258], ACT.Exp).then_inc(S("lam_exp"), 1)

                def diff_squares(i):
                    act.wait_ge(S("o_copied"), 8 + 12 * layer + 2 * i + 2)
                    act.activation(sq[:, 2 * i:2 * i + 2, :], od[:, 2 * i:2 * i + 2, :], ACT.Square)\
                        .then_inc(S("od_sq_ready"), 1)

                def diff_root(i):
                    v = sq[:, 4 + 2 * i:6 + 2 * i, :]
                    root("od_var_ready", 2 * layer + i + 1, v, v, "od_std_ready")

                def mixed_hi(waited, value, lo, hi):
                    act.wait_ge(S(waited), value)
                    settled(act)
                    act.copy(h_hi[:, lo:hi, :], h_t[:, lo:hi, :]).then_inc(S("mix_hi_ready"), 1)

                attention("layer", 8 + 16 * layer, 8 + 12 * layer,
                          {9: lambda: diff_squares(0), 11: lambda: diff_root(0),
                           13: lambda: diff_squares(1), 15: lambda: diff_root(1),
                           17: lambda: mixed_hi("o_copied", 8 + 12 * layer + 8, 0, 2),
                           18: lambda: mixed_hi("diff_made", layer + 1, 4, 8)})
                mixed_hi("o_copied", 8 + 12 * layer + 10, 2, 3)
                mixed_hi("o_copied", 8 + 12 * layer + 12, 3, 4)
                split_step(layer, MIX_AT + V_SLOTS + 6)
                split_step(layer, MIX_AT + V_SLOTS + 7)
                norm(3 * layer + 3)
                swiglu(layer, 1)
                own.restart()
            norm(3 * LAYERS + 1, split=False)

        @block.vector
        def _(dve):
            own = Chain(dve, S("dve_own"))
            tt, ts, stt = dve.tensor_tensor, dve.tensor_scalar, dve.scalar_tensor_tensor

            def over(a, n, where=1):
                v = a.unsqueeze(where)
                return v.to_broadcast([*v.shape[:where], n, *v.shape[where + 1:]])

            def attention(kind, s0, o0, extra=None):
                scores, outs = attention_units(kind)

                def scores_in(s):
                    what, h = scores[s]
                    dve.wait_ge(S("score_done"), s0 + s + 1)
                    if s >= 4:
                        o = next(i for i, (end, _) in enumerate(outs) if end >= s - 4)
                        dve.wait_ge(S("turned"), o0 + o + 1)
                    settled(dve)
                    for j in range(TT):
                        add = bias[:, h, P * (1 - j):P * (1 - j) + T] if what == "m" else \
                            late("causal")[:, j * T:(j + 1) * T]
                        m = dve.tensor_tensor_reduce(out=probs[:, s % 4, j, :], in0=ps[s % 2][:, j * T:(j + 1) * T],
                                                     in1=add, scale=1.0, scalar=-3e38, op0=ALU.add, op1=ALU.max,
                                                     accum_out=small[:, s % 4, 0, j:j + 1])
                    m.then_inc(S("score_read"), 1)
                    dve.wait_ge(S("score_read"), s0 + s + 1)
                    ts(small[:, s % 4, 1, :], small[:, s % 4, 0, :], -1.0, None, ALU.mult)\
                        .then_inc(S("negmax_ready"), 1)

                def reciprocals(s):
                    what, c = scores[s]
                    dve.wait_ge(S("exp_ready"), s0 + s + 1)
                    r = small[:, s % 4, 3, :]
                    if what == "d" and c % 2:
                        own(dve.reciprocal(r, small[:, s % 4, 2, :]))
                        ts(r, r, lams[:, 4:5], None, ALU.mult).then_inc(S("recip_ready"), 1)
                    else:
                        dve.reciprocal(r, small[:, s % 4, 2, :]).then_inc(S("recip_ready"), 1)

                def output(o):
                    what, h = outs[o][1]
                    dve.wait_ge(S("o_ready"), o0 + o + 1)
                    if what == "d":
                        dst, po, w = od[:, h, :], 0, P
                    else:
                        po, w = DH * (h % 2), DH
                        dst = h_t[po:po + w, h // 2 + (4 if what == "m" else 0), :]
                    dve.tensor_copy(dst, ps[4 + o % 2][po:po + w, 0:T]).then_inc(S("o_copied"), 1)

                for s in range(len(scores) + OUTPUT):
                    if s < len(scores):
                        scores_in(s)
                    if 1 <= s <= len(scores):
                        reciprocals(s - 1)
                    for o, (end, _) in enumerate(outs):
                        if end == s - OUTPUT:
                            output(o)
                    if extra and s in extra:
                        extra[s]()

            def residual(value, x_by, by):
                for b in range(PAIRS):
                    dve.wait_ge(S("wide_done"), PAIRS * (value - 1) + b + 1)
                    settled(dve)
                    xb, pb = x_t[:, 2 * b:2 * b + 2, :], halves(4 + b)
                    if by == 1.0:
                        m = stt(xb, xb, x_by, pb, ALU.mult, ALU.add)
                    else:
                        m = stt(xb, pb, by, xb, ALU.mult, ALU.add)
                    m.then_inc(S("x_updates"), 1)

            def rms_stat(value, bank=0):
                dve.wait_ge(S("sum_ready"), 4 + value)
                ts(stat[:, 1, :], ps[bank][:, 0:T], 1.0 / D, EPS, ALU.mult, ALU.add).then_inc(S("var_ready"), 1)
                dve.wait_ge(S("std_ready"), 2 + value)
                own(dve.reciprocal(stat[:, 3, :], stat[:, 2, :]))

            def norm(value, gain_of):
                rms_stat(value)
                for b in range(KB):
                    stt(h_t[:, b, :], x_t[:, b, :], gain_of(b), stat[:, 3, :], ALU.mult, ALU.mult)\
                        .then_inc(S("h_made"), 1)

            def lo_part(layer, q, part, more=0, counts=1):
                lo, hi = (0, PART_A * P) if part == "A" else (PART_A * P, SLOT)
                dve.wait_ge(S("hi_ready"), 2 * LAYER_SLOTS * layer + 2 * q + (1 if part == "A" else 2) + 2 * more)
                settled(dve)
                tt(w_lo[:, q % 2, lo:hi], ring[:, RAW[q % 4], lo:hi], w_hi[:, q % 2, lo:hi].bitcast(F32),
                   ALU.subtract).then_inc(S("lo_ready"), counts)

            def split_step(layer, q, more=0):
                token_major = MIX_AT <= q < MIX_AT + V_SLOTS
                if not token_major:
                    lo_part(layer, q, "B", more)
                if q < LAYER_SLOTS - 1:
                    lo_part(layer, q + 1, "A", more, 2 if token_major else 1)

            def layer_norm(n, g):
                dve.wait_ge(S("x_updates"), PAIRS * n)
                dve.wait_ge(S("sum_ready"), 2 * n - 1)
                own(ts(stat[:, 0, :], ps[0][:, 0:T], 1.0 / D, None, ALU.mult))
                for p in range(PAIRS):
                    pair = x_t[:, 2 * p:2 * p + 2, :]
                    tt(pair, pair, over(stat[:, 0, :], 2), ALU.subtract).then_inc(S("centred"), 1)
                dve.wait_ge(S("sum_ready"), 2 * n)
                ts(stat[:, 1, :], ps[1][:, 0:T], 1.0 / D, EPS, ALU.mult, ALU.add).then_inc(S("var_ready"), 1)
                dve.wait_ge(S("std_ready"), n)
                own(dve.reciprocal(stat[:, 3, :], stat[:, 2, :]))
                for k in range(KB):
                    stt(x_t[:, k, :], x_t[:, k, :], param(g, k), stat[:, 3, :], ALU.mult, ALU.mult)\
                        .then_inc(S("scaled"), 1)

            dve.wait_ge(S("params_loaded"), 16)
            l0, l1 = param("lb", 0, 4), param("lb", 4, 4)
            own(tt(lbs[:, 0:4], l0, l1, ALU.max))
            tt(lbs[:, 4:8], l0, lbs[:, 0:4], ALU.subtract)
            tt(lbs[:, 8:12], l1, lbs[:, 0:4], ALU.subtract).then_inc(S("lb_shifted"), 1)
            ts(negb[:], param("b_in", 4, 4), -1.0, None, ALU.mult)
            dve.wait_ge(S("lb_exp"), 1)
            own(tt(lbs[:, 0:4], lbs[:, 4:8], lbs[:, 8:12], ALU.add))
            own(dve.reciprocal(lbs[:, 8:12], lbs[:, 0:4]))
            own(tt(lbs[:, 12:16], lbs[:, 4:8], lbs[:, 8:12], ALU.mult))
            own(ts(lbs[:, 16:20], lbs[:, 12:16], -1.0, 1.0, ALU.mult, ALU.add))
            ts(lbs[:, 20:24], param("b_in", 12, 4), DH ** -0.5, None, ALU.mult).then_inc(S("lb_ready"), 1)
            dve.wait_ge(S("bias_row_done"), 1)
            dve.tensor_copy(bias_row[:, 0:T], ps[5][0:8, 0:T]).then_inc(S("bias_row_ready"), 1)

            dve.wait_ge(S("proj_read"), 4)
            for h in range(HG_HEADS):
                ts(f_hg[:, h, :], f_hg[:, h, :], lbs[:, 16 + h:17 + h], lbs[:, 12 + h:13 + h], ALU.mult, ALU.add)
                m = ts(k_hg[:, h, :], k_hg[:, h, :], lbs[:, 16 + h:17 + h], None, ALU.mult)
            own(m)

            def subs(a):
                return a.rearrange("p h (n t) -> p (h n) t", t=SUB)

            q, f, k, g = subs(q_hg), subs(f_hg), subs(k_hg), subs(grow)
            dve.wait_ge(S("band_p_zero"), 1)
            for d in range(SUB):
                p = subs(band_p[:, d % 2, :, :])
                if d:
                    dve.wait_ge(S("band_p_ready"), d)
                if d == 1:
                    own(tt(g[:, :, 1:], q[:, :, 1:], f[:, :, 1:], ALU.mult))
                elif d > 1:
                    own(tt(g[:, :, d:], g[:, :, d:], f[:, :, 1:SUB + 1 - d], ALU.mult))
                    dve.wait_ge(S("band_done"), d - 1)
                now = q if d == 0 else g
                tt(p[:, :, 0:SUB - d], now[:, :, d:], k[:, :, 0:SUB - d], ALU.mult).then_inc(S("band_p_ready"), 1)
            own(dve.tensor_copy(g[:, :, 0], f[:, :, 0]))
            for t in range(1, SUB):
                own(tt(g[:, :, t], g[:, :, t - 1], f[:, :, t], ALU.mult))
            tt(q, q, g, ALU.mult)
            own(tt(k[:, :, SUB - 2], k[:, :, SUB - 2], f[:, :, SUB - 1], ALU.mult))
            own(dve.tensor_copy(decays[:, 0, :], f[:, :, SUB - 1]))
            for n, t in enumerate(range(SUB - 3, -1, -1)):
                now = decays[:, (n + 1) % 2, :]
                own(tt(now, decays[:, n % 2, :], f[:, :, t + 1], ALU.mult))
                m = tt(k[:, :, t], k[:, :, t], now, ALU.mult)
            own(m)
            dve.wait_ge(S("band_done"), SUB)
            dve.tensor_copy(band[:], ps[4][:, 0:8 * SUB].rearrange("p (n d) -> p n d", n=8))\
                .then_inc(S("band_copied"), 1)
            dve.wait_ge(S("kdec_zero"), 1)
            for i in range(1, NSUB):
                if i >= 3:
                    dve.wait_ge(S("earlier_done"), i - 2)
                new, old = kdec[:, i % 2, :, :], kdec[:, (i - 1) % 2, :, :]
                at = SUB * (i - 1)
                if i > 1:
                    for h in range(HG_HEADS):
                        ts(new[:, h, 0:at], old[:, h, 0:at], grow[:, h, at + SUB - 1:at + SUB], None, ALU.mult)
                dve.tensor_copy(new[:, :, at:at + SUB], k_hg[:, :, at:at + SUB]).then_inc(S("kdec_ready"), 1)
                dve.wait_ge(S("kdec_ready"), i)
                if i == 1:
                    dve.wait_ge(S("band_copied"), 1)
                    mask = const("band").rearrange("p (d t) -> p d t", d=SUB)
                    own(tt(wide, over(band[:], SUB, 3), over(mask, 8, 1), ALU.mult))
                    own(dve.tensor_reduce(band[:], wide.rearrange("p n d t -> p n t d"), AX.X, ALU.add))
                    intra = stat[:, :, :].rearrange("p a (b t) -> p (a b t)", t=SUB)\
                        .rearrange("p (n b t) -> p n b t", n=8, t=SUB)
                    own(tt(intra, over(band[:], P // SUB, 2), over(over(const("blk"), SUB, 2), 8, 1), ALU.mult))
                    own(dve.memset(hg_scores, 0.0))
            dve.wait_ge(S("earlier_done"), NSUB - 1)
            for h in range(HG_HEADS):
                dve.tensor_copy(hg_scores[:, h, 0, SUB:], ps[4 + h][:, SUB:T])
                m = dve.tensor_copy(hg_scores[:, h, 1, P + SUB:], ps[4 + h][:, T + P + SUB:2 * T])
            own(m)
            flat = stat[:, :, :].rearrange("p a t -> p (a t)").rearrange("p (h j t) -> p h j t", h=4, j=TT)
            for j in range(TT):
                s = hg_scores[:, :, j, j * P:(j + 1) * P]
                m = tt(s, s, flat[:, :, j, :], ALU.add)
            m.then_inc(S("hg_scores_ready"), 1)

            def hg_variance():
                dve.wait_ge(S("hg_sum_ready"), 1)
                for i in range(2):
                    m = ts(sq[:, 4 + 2 * i:6 + 2 * i, :], halves(6 + i), 1.0 / P, EPS, ALU.mult, ALU.add)
                m.then_inc(S("hg_var_ready"), 1)

            def hg_norm(h):
                if h == 0:
                    dve.wait_ge(S("hg_std_ready"), 1)
                own(dve.reciprocal(sq[:, 4 + h, :], sq[:, 4 + h, :]))
                own(tt(grow[:, h, :], grow[:, h, :], sq[:, 4 + h, :], ALU.mult))
                own.mark(stt(h_t[:, h, :], grow[:, h, :], param("hg_g", h), g_hg[:, h, :], ALU.mult, ALU.mult))

            dve.wait_ge(S("bias_loaded"), 16)
            attention("moba", 0, 0, {2: hg_variance, 4: lambda: hg_norm(0), 5: lambda: hg_norm(1),
                                     6: lambda: hg_norm(2), 7: lambda: hg_norm(3)})
            own.wait()

            for j in range(KB):
                dve.wait_ge(S("ab_done"), j + 1)
                own(tt(sq[:, j, :], ps[j % 4][:, 0:T], gates[:, j, :], ALU.mult))
                own(tt(stat[:, j % 2, :], ps[j % 4][:, T:2 * T], gates[:, KB + j, :], ALU.mult))
                tt(sq[:, j, :], sq[:, j, :], stat[:, j % 2, :], ALU.add).then_inc(S("mixed_ready"), 1)
            residual(1, ALPHA, 1.0)
            layer_norm(1, "ln1_g")

            def table(at, n):
                return routing[:, at:at + TT * n].rearrange("p (j n) -> p j n", j=TT)

            logits, e1, e2 = table(64, ROUTED), table(192, EXPERTS), table(256, EXPERTS)
            masked, keyed, pos = table(320, EXPERTS), table(384, EXPERTS), table(448, EXPERTS)
            chosen, keyed_g, shifted = table(512, GROUPS), table(544, GROUPS), table(896, GROUPS)
            penalty = table(576, GROUPS)
            gmax, rank, gsum, pgrp = (routing[:, a:a + TT] for a in (608, 610, 612, 614))
            top1, top2, den, w1, w2 = (routing[:, a:a + TT] for a in (616, 618, 620, 622, 624))
            pos1, pos2, second = (routing[:, a:a + TT] for a in (626, 628, 960))
            assigned = table(0, EXPERTS)

            def first_of(values, best, rev, key, where):
                own(tt(key, values, over(best, values.shape[2], 2), ALU.is_equal))
                own(tt(key, key, over(rev, TT), ALU.mult))
                own(dve.tensor_reduce(rank, key, AX.X, ALU.max))
                own(tt(where, key, over(rank, values.shape[2], 2), ALU.is_equal))

            dve.wait_ge(S("logits_done"), 1)
            own(dve.tensor_copy(logits, ps[2][:, 0:TT * ROUTED].rearrange("p (j n) -> p j n", j=TT)))
            lg = logits[:, :, 0:GROUPS]
            own(dve.tensor_reduce(gmax, lg, AX.X, ALU.max))
            tt(shifted, lg, over(gmax, GROUPS, 2), ALU.subtract).then_inc(S("group_shifted"), 1)
            first_of(lg, gmax, const("rev_group"), keyed_g, chosen)
            own(ts(penalty, chosen, -1.0, -NEG, ALU.add, ALU.mult))
            le = logits[:, :, GROUPS:].rearrange("p j (g e) -> p j g e", g=GROUPS)
            me = masked.rearrange("p j (g e) -> p j g e", g=GROUPS)
            own(tt(me, le, over(chosen, PER_GROUP, 3), ALU.mult))
            own(tt(me, me, over(penalty, PER_GROUP, 3), ALU.add))
            own(dve.tensor_reduce(top1, masked, AX.X, ALU.max))
            first_of(masked, top1, const("rev_expert"), keyed, e1)
            own(stt(masked, e1, 3.0 * NEG, masked, ALU.mult, ALU.add))
            own(dve.tensor_reduce(top2, masked, AX.X, ALU.max))
            tt(second, top2, top1, ALU.subtract).then_inc(S("second_shifted"), 1)
            first_of(masked, top2, const("rev_expert"), keyed, e2)
            tt(assigned, e1, e2, ALU.add).then_inc(S("assigned_ready"), 1)
            dve.wait_ge(S("group_exp"), 1)
            own(dve.tensor_reduce(gsum, shifted, AX.X, ALU.add))
            own(dve.reciprocal(pgrp, gsum))
            dve.wait_ge(S("second_exp"), 1)
            own(ts(den, second, 1.0, None, ALU.add))
            own(dve.reciprocal(den, den))
            own(tt(w1, pgrp, den, ALU.mult))
            own(tt(w2, w1, second, ALU.mult))
            dve.wait_ge(S("counts_done"), 1)
            cnt, passes = counts_t[:, 0:P], counts_t[:, P:2 * P]
            own(dve.tensor_copy(cnt, ps[3][0:EXPERTS, P:2 * P]))
            assert T == 2 * WIN
            ts(passes, cnt, WIN + 0.5, 1.0, ALU.is_gt, ALU.add).then_inc(S("counts_ready"), 1)
            dve.wait_ge(S("starts_done"), 1)
            own(dve.tensor_copy(routing[0:1, 672:672 + 3 * EXPERTS], ps[2][0:1, 128:128 + 3 * EXPERTS]))
            starts_f, passes_f, before_f = (routing[0:1, 672 + i * EXPERTS:672 + (i + 1) * EXPERTS] for i in range(3))
            packed = routing[0:1, 768:768 + EXPERTS]
            own(stt(packed, starts_f, 64.0, before_f, ALU.mult, ALU.add))
            own(stt(packed, packed, 4.0, passes_f, ALU.mult, ALU.add))
            dve.tensor_copy(meta[:], routing[0:1, 672:672 + 4 * EXPERTS]).then_inc(S("meta_ready"), 1)
            own(dve.tensor_copy(routing[:, 640:672], ps[2][:, 128:160]))
            own(tt(pos, ps[3][:, 0:TT * EXPERTS].rearrange("p (j n) -> p j n", j=TT),
                   over(routing[:, 640:672], TT), ALU.add))
            for e, where in ((e1, pos1), (e2, pos2)):
                own(tt(keyed, e, pos, ALU.mult))
                own(dve.tensor_reduce(where, keyed, AX.X, ALU.add))
            dve.wait_ge(S("iota_loaded"), 16)
            for j in range(TT):
                p1, p2 = pos1[:, j:j + 1], pos2[:, j:j + 1]
                own(ts(pick[:, j, :], iota, p1, None, ALU.is_equal))
                m = stt(pick[:, j, :], iota, p2, pick[:, j, :], ALU.is_equal, ALU.add)
            m.then_inc(S("pick_ready"), 1)
            for j in range(TT):
                p1, p2 = pos1[:, j:j + 1], pos2[:, j:j + 1]
                own(ts(mixw[:, j, :], iota, p1, w1[:, j:j + 1], ALU.is_equal, ALU.mult))
                own(ts(mixw_2[:, j, :], iota, p2, w2[:, j:j + 1], ALU.is_equal, ALU.mult))
                m = tt(mixw[:, j, :], mixw[:, j, :], mixw_2[:, j, :], ALU.add)
            m.then_inc(S("mixw_ready"), 1)
            dve.wait_ge(S("mixw_turned"), 1)
            for i in range(2):
                m = dve.tensor_copy(mixw_t[:, 2 * i:2 * i + 2, :], halves(i))
            m.then_inc(S("mixw_t_ready"), 1)
            dve.wait_ge(S("mixw_ready"), 1)

            with dve.Fori(0, EXPERTS) as e:
                start = dve.value_load(meta[0:1, bass.ds(e, 1)], min_val=0, max_val=ASSIGNED)
                passes_r = dve.value_load(meta[0:1, bass.ds(EXPERTS + e, 1)], min_val=1, max_val=T // WIN)
                before = dve.value_load(meta[0:1, bass.ds(2 * EXPERTS + e, 1)], min_val=0,
                                        max_val=EXPERTS + ASSIGNED // WIN)
                with dve.Fori(0, passes_r) as w:
                    at = nc.s_assert_within(start + WIN * w, 0, ASSIGNED,
                                            skip_runtime_bounds_check_because="it begins at an assigned token")
                    for side in range(2):
                        dve.wait_ge(S("moe_silu"), 2 * before + 2 * w + side + 1)
                        tt(two["hid"][:, 2 * side:2 * side + 2, :],
                           two["sg"][:, side * T:(side + 1) * T].rearrange("p (k n) -> p k n", k=2),
                           ps[side][:, T:2 * T].rearrange("p (k n) -> p k n", k=2), ALU.mult)\
                            .then_inc(S("hid_ready"), 1)
                    dve.wait_ge(S("down_done"), before + w + 1)
                    for half in range(2):
                        m = dve.tensor_copy(ys[:, 4 * half:4 * half + 4, bass.ds(at, WIN)],
                                            ps[2 + half][:, :].rearrange("p (k n) -> p k n", k=4))
                    m.then_inc(S("ys_written"), 1)
            dve.memset(lams[:, 7:8], 0.0).then_inc(S("moe_done"), 1)
            residual(2, ALPHA, 1.0)
            layer_norm(2, "ln2_g")

            dve.sem_inc(S("hid_made"), 4)
            dve.wait_ge(S("late_loaded"), 16)

            def swiglu(layer, f):
                at = FFN2_AT * f

                def hidden(c, more):
                    n = 2 * CHUNKS * layer + CHUNKS * f + c + more
                    hid = three["hid"][:, c % 2, :]
                    dve.wait_ge(S("silu_done"), n + 1)
                    dve.wait_ge(S("hid_made"), n + 3)
                    settled(dve)
                    tt(hid, three["sg"][:, c % 2, :], ps[c % 4][:, T:2 * T], ALU.mult).then_inc(S("hid_whole"), 1)
                    dve.wait_ge(S("hid_whole"), n + 1)
                    settled(dve)
                    dve.tensor_copy(hid_hi[:, c % 2, :], hid).then_inc(S("hid_hi_made"), 1)
                    dve.wait_ge(S("hid_hi_made"), n + 1)
                    settled(dve)
                    tt(hid_lo[:, c % 2, :], hid, hid_hi[:, c % 2, :].bitcast(F32), ALU.subtract)\
                        .then_inc(S("hid_made"), 1)
                    if c < CHUNKS - 1:
                        split_step(layer, at + c + 1, more)
                split_step(layer, at)
                over_chunks(dve, hidden)

            own.restart()
            with dve.Fori(0, LAYERS) as layer:
                own.mark(dve.tensor_copy(cur[:, 0:l_n], params[:, bass.ds(p_at["layers"][0] + l_n * layer, l_n)]))
                own(dve.tensor_copy(cur[:, l_n:l_n + 2], consts[:, bass.ds(c_at["lam_init"][0] + 2 * layer, 2)]))
                at = l_at["lam"][0]
                for i in range(2):
                    m = tt(lams[0:DH, i:i + 1], cur[0:DH, at + 2 * i:at + 2 * i + 1],
                           cur[0:DH, at + 2 * i + 1:at + 2 * i + 2], ALU.mult)
                m.then_inc(S("lam_ready"), 1)
                norm(3 * layer + 1, lambda b: gain("ffn1", b))
                swiglu(layer, 0)
                residual(3 + 3 * layer, 1.0, 0.5)
                norm(3 * layer + 2, lambda b: gain("mix", b))
                split_step(layer, MIX_AT)
                dve.wait_ge(S("forget_done"), layer + 1)
                z = ffs[:, 0, :, :]
                own(dve.tensor_copy(z, ps[4][:, 0:TT * 8].rearrange("p (j n) -> p j n", j=TT)))
                stt(ffs[:, 1, :, :], z, -1.0, z, ALU.mult, ALU.min).then_inc(S("forget_shifted"), 1)
                split_step(layer, MIX_AT + 1)
                dve.wait_ge(S("forget_log"), layer + 1)
                stt(ffs[:, 5, :, :], z, 0.0, ffs[:, 4, :, :], ALU.min, ALU.subtract).then_inc(S("log_f_ready"), 1)

                def rope(r):
                    dve.wait_ge(S("rotated"), 4 * layer + r + 1)
                    pair = qk[:, 2 * r:2 * r + 2, :]
                    turned = rotated[:, r % 2, :, :]
                    own.mark(tt(turned, halves(6 + r % 2), over(late("sin"), 2), ALU.mult))
                    own(tt(pair, pair, over(late("cos"), 2), ALU.mult))
                    tt(pair, pair, turned, ALU.add).then_inc(S("rope_done"), 1)

                for u in range(1, LAYER_UNITS):
                    if 6 <= u < 10:
                        rope(u - 6)
                    for q in MIX_STEPS.get(u, ()):
                        split_step(layer, q)
                dve.wait_ge(S("cum_done"), layer + 1)
                ts(ncum[0:8, :], ps[5][0:8, 0:T], -1.0, None, ALU.mult).then_inc(S("ncum_ready"), 1)
                dve.wait_ge(S("lam_exp"), layer + 1)
                own(stt(lams[:, 4:5], lams[:, 3:4], cur[:, l_n:l_n + 1], lams[:, 2:3], ALU.subtract, ALU.subtract))

                def diff_variance(i):
                    dve.wait_ge(S("od_sum_ready"), 2 * layer + i + 1)
                    ts(sq[:, 4 + 2 * i:6 + 2 * i, :], halves(6 + i), 1.0 / P, EPS, ALU.mult, ALU.add)\
                        .then_inc(S("od_var_ready"), 1)

                def diff_norm(h):
                    if h % 2 == 0:
                        dve.wait_ge(S("od_std_ready"), 2 * layer + h // 2 + 1)
                        settled(dve)
                    own(dve.reciprocal(sq[:, 4 + h, :], sq[:, 4 + h, :]))
                    own(tt(od[:, h, :], od[:, h, :], sq[:, 4 + h, :], ALU.mult))
                    m = ts(h_t[:, 4 + h, :], od[:, h, :], gain("subln", 0), cur[:, l_n + 1:l_n + 2], ALU.mult, ALU.mult)
                    if h < 3:
                        own.mark(m)
                    else:
                        m.then_inc(S("diff_made"), 1)

                def mixed_lo(n, lo, hi):
                    dve.wait_ge(S("mix_hi_ready"), 4 * layer + n)
                    settled(dve)
                    tt(h_lo[:, lo:hi, :], h_t[:, lo:hi, :], h_hi[:, lo:hi, :].bitcast(F32), ALU.subtract)\
                        .then_inc(S("mix_in_ready"), 1)

                attention("layer", 8 + 16 * layer, 8 + 12 * layer,
                          {10: lambda: diff_variance(0), 11: lambda: diff_norm(0), 12: lambda: diff_norm(1),
                           14: lambda: diff_variance(1), 16: lambda: diff_norm(2), 17: lambda: diff_norm(3),
                           18: lambda: mixed_lo(1, 0, 2), 19: lambda: mixed_lo(2, 4, 8)})
                own.wait()
                mixed_lo(3, 2, 3)
                mixed_lo(4, 3, 4)
                split_step(layer, MIX_AT + V_SLOTS + 6)
                split_step(layer, MIX_AT + V_SLOTS + 7)
                residual(4 + 3 * layer, 1.0, 1.0)
                norm(3 * layer + 3, lambda b: gain("ffn2", b))
                swiglu(layer, 1)
                residual(5 + 3 * layer, 1.0, 0.5)
                own.restart()
            norm(3 * LAYERS + 1, lambda b: param("final", b))


def constant_tables():
    idx = np.arange(P)
    t = np.arange(T)
    bucket = np.arange(T, dtype=np.int64)
    half = BUCKETS // 2
    d = np.maximum(bucket, 1).astype(np.float32)
    log_part = half + (np.log(d / np.float32(half)) / np.float32(math.log(MAX_DIST / half))
                       * np.float32(BUCKETS - half)).astype(np.int32)
    bucket = np.where(bucket < half, bucket, np.minimum(log_part, BUCKETS - 1))
    by_distance = (bucket[None, ::-1] == np.arange(BUCKETS)[:, None])
    rot = np.zeros((P, P))
    for m in range(P):
        if m % DH < DH // 2:
            rot[m + DH // 2, m] = -1.0
        else:
            rot[m - DH // 2, m] = 1.0
    band = (np.arange(SUB)[None, None, :] == (idx % SUB)[:, None, None] + np.arange(SUB)[None, :, None])
    init = [0.8 - 0.6 * math.exp(-0.3 * n) for n in range(LAYERS)]
    tables = {
        "ident": np.eye(P), "ones": np.ones((P, P)), "tri": idx[:, None] <= idx[None, :],
        "tri_strict": idx[:, None] < idx[None, :], "rot": rot, "band": band.reshape(P, -1),
        "blk": (idx // SUB)[:, None] == np.arange(P // SUB)[None, :],
        "rev_group": np.tile(np.arange(GROUPS, 0, -1), (P, 1)),
        "rev_expert": np.tile(np.arange(EXPERTS, 0, -1), (P, 1)),
        "bucket": np.concatenate([by_distance, np.zeros((P - BUCKETS, T))]),
        "lam_init": np.tile(np.array([[v, 1.0 - v] for v in init]).reshape(1, -1), (P, 1)),
    }
    inv = (1.0 / (np.float32(10000.0) ** (np.arange(0, DH, 2, dtype=np.float32) / np.float32(DH)))).astype(np.float32)
    angle = np.concatenate([t.astype(np.float32)[:, None] * inv[None, :]] * 2, axis=1)
    causal = np.stack([np.where(t[None, :] <= (idx + j * P)[:, None], 0.0, NEG) for j in range(TT)], 1)
    late = {"cos": np.tile(np.cos(angle).T, (2, 1)), "sin": np.tile(np.sin(angle).T, (2, 1)),
            "causal": causal.reshape(P, -1)}
    iota = np.tile(np.arange(ASSIGNED), (P, 1))
    pack = lambda names, of: np.concatenate([np.asarray(of[n], np.float32) for n in names], axis=1)
    return pack(CONSTS, tables), pack(("cos", "sin", "causal"), late), iota.astype(np.float32)


def sub_blocks(w):
    k, n = w.shape
    return w.reshape(k // P, P, n // P, P).transpose(1, 2, 0, 3)


def flat(*parts):
    return np.concatenate([p.reshape(P, -1) for p in parts], axis=1)


def slots(a, n):
    full = np.zeros((P, n * SLOT), np.float32)
    full[:, :a.shape[1]] = a
    return full.reshape(P, n, SLOT).transpose(1, 0, 2)


def token_major(w):
    out = []
    for v in range(w.shape[1] // VCOLS):
        part = w[:, v * VCOLS:(v + 1) * VCOLS].reshape(KB, P, VCOLS).transpose(1, 0, 2)
        out.append(slots(flat(part), 1))
    return np.concatenate(out)


def columns(v):
    return v.reshape(-1, P).T


FORGET = slice(3 * MB_HEADS * DH, 3 * MB_HEADS * DH + 8)


def layouts(i):
    w, b = i["w_in"][0], i["b_in"][0]
    at = {}
    first = 0
    for name, n in (("q", 512), ("f", 512), ("v", 512), ("g", 512), ("mq", 512), ("mk", 512), ("mv", 512),
                    ("ga", 1024), ("gb", 1024)):
        at[name] = slice(first, first + n)
        first += n
    early, later = ("q", "f", "g"), ("mq", "mk", "ga", "gb")
    ab = np.concatenate([sub_blocks(i["w_proj_a"][0]), sub_blocks(i["w_proj_b"][0])], axis=2)
    router = np.concatenate([i["w_group"][0], i["w_expert"][0]], axis=1).reshape(KB, P, ROUTED).transpose(1, 0, 2)
    first_w = np.concatenate([
        slots(flat(*[sub_blocks(w[:, at[n]]) for n in early]), 4),
        token_major(np.concatenate([w[:, at["v"]], w[:, at["mv"]]], axis=1)),
        slots(flat(*[sub_blocks(w[:, at[n]]) for n in later]), 8),
        slots(flat(ab, sub_blocks(i["w_out"][0]), router), 6)])
    moe_w = np.empty((MOE_SLOTS, P, SLOT), np.float32)
    for e in range(EXPERTS):
        up, down = sub_blocks(i["w_gate_up"][0, e]), sub_blocks(i["w_down"][0, e])
        moe_w[4 * e:4 * e + 4] = slots(flat(up[:, 0:2], up[:, 4:6], up[:, 2:4], up[:, 6:8],
                                            down[:, :, 0:2], down[:, :, 2:4]), 4)
    layer_w = np.empty((LAYERS * LAYER_SLOTS, P, SLOT), np.float32)
    for n in range(LAYERS):
        at_n = n * LAYER_SLOTS
        for first, name in ((0, "ffn1"), (FFN2_AT, "ffn2")):
            gu, down = i[f"{name}_w_gate_up_2"][n], i[f"{name}_w_down_2"][n]
            gate, up = sub_blocks(gu[:, :D_FF]), sub_blocks(gu[:, D_FF:])
            for c in range(CHUNKS):
                layer_w[at_n + first + c] = flat(gate[:, c], up[:, c], down[c * P:(c + 1) * P])
        w2 = i["w_in_2"][n]
        fq, fk, fv, _, dq, dk, dv = np.split(w2, np.cumsum([512, 512, 512, 8, 512, 512]), axis=1)
        m = at_n + MIX_AT
        layer_w[m:m + V_SLOTS] = token_major(np.concatenate([fv, dv], axis=1))
        layer_w[m + V_SLOTS:m + V_SLOTS + 8] = slots(
            flat(*[sub_blocks(v) for v in (dq, dk, fq, fk, i["w_out_2"][n])]), 8)
    b_in = np.concatenate([columns(b[at[n]]) for n in early + later], axis=1)
    rel = np.zeros((P, MB_HEADS), np.float32)
    rel[:BUCKETS] = i["rel_bias"]
    per_layer = []
    for n in range(LAYERS):
        lam = np.zeros((P, 4), np.float32)
        for c, name in enumerate(("lambda_q1_2", "lambda_k1_2", "lambda_q2_2", "lambda_k2_2")):
            lam[:DH, c] = i[name][n]
        per_layer += [columns(i["ffn1_norm_2"][n]), columns(i["mix_norm_2"][n]), columns(i["ffn2_norm_2"][n]),
                      columns(i["diff_subln_2"][n]), lam]
    params = np.concatenate([
        b_in, columns(i["lb_logits"][0]), columns(i["lb_logits"][1]), columns(i["hg_norm_g"][0]),
        columns(i["ln1_g"][0]), columns(i["ln1_b"][0]), columns(i["ln2_g"][0]), columns(i["ln2_b"][0]),
        rel, columns(i["final_norm_2"]), *per_layer], axis=1)
    rows = np.concatenate([i["b_group"][0], i["b_expert"][0], i["forget_bias_2"].reshape(-1)])[None]
    b_v = np.concatenate([b[at["v"]], b[at["mv"]]])[None]
    x = i["x"][0].T.reshape(KB, P, T).transpose(1, 0, 2)
    consts, late, iota = constant_tables()
    late = np.concatenate([late] + [i["w_in_2"][n][:, FORGET].reshape(KB, P, 8).transpose(1, 0, 2).reshape(P, -1)
                                    for n in range(LAYERS)], axis=1)
    return {"x": x, "first_w": first_w, "moe_w": moe_w, "layer_w": layer_w, "consts": consts, "late": late,
            "iota": iota, "params": params, "rows": rows, "b_v": b_v}


def kernel(**inputs):
    import concourse.bacc as bacc
    from concourse.bass_utils import run_bass_kernel_spmd

    nc = bacc.Bacc("TRN2", target_bir_lowering=False, num_devices=1)
    arrays = {f"{name}_dram": np.ascontiguousarray(a)
              for name, a in layouts({k: np.asarray(v) for k, v in inputs.items()}).items()}
    args = [nc.dram_tensor(name, a.shape, F32, kind="ExternalInput").ap() for name, a in arrays.items()]
    out = nc.dram_tensor("out_dram", (P, KB, T), F32, kind="ExternalOutput").ap()
    program(nc, *args, out)
    r = run_bass_kernel_spmd(nc, [arrays], core_ids=[0])
    y = r.results[0]["out_dram"]
    return np.ascontiguousarray(y.transpose(1, 0, 2).reshape(D, T).T).reshape(1, T, D)
```
